# Optimizing a Trainium2 kernel written in Bass

```python
import math
import jax, jax.numpy as jnp
from jax import lax
import numpy as np

D_MODEL = 2048
BATCH = 1
SEQ = 512
DEPTH = 1

D_MIX = D_MODEL
MLA_HEADS = 8
MLA_NOPE_DIM = 128
MLA_ROPE_DIM = 64
MLA_V_DIM = 128
MLA_WIDTH = MLA_HEADS * MLA_V_DIM
Q_LORA_RANK = 512
KV_LORA_RANK = 256
CONV_GROUPS = 8
CONV_WIDTH = D_MIX - MLA_WIDTH
CONV_K = 3
FFN_DIM = 5632
FFN_CONV_K = 3
ROPE_THETA = 10000.0
Q_BLOCK = 128
LN_EPS = 1e-5
RMS_EPS = 1e-6
DEEPNORM_ALPHA = (2.0 * DEPTH) ** 0.25
DEEPNORM_BETA = (8.0 * DEPTH) ** -0.25
IN_PROJ_DIM = Q_LORA_RANK + KV_LORA_RANK + MLA_ROPE_DIM + 3 * CONV_WIDTH
IN_SPLITS = (Q_LORA_RANK,
             Q_LORA_RANK + KV_LORA_RANK,
             Q_LORA_RANK + KV_LORA_RANK + MLA_ROPE_DIM,
             Q_LORA_RANK + KV_LORA_RANK + MLA_ROPE_DIM + CONV_WIDTH,
             Q_LORA_RANK + KV_LORA_RANK + MLA_ROPE_DIM + 2 * CONV_WIDTH)

kernel_name = "hymba_mla_shortconv_convffn_deepnorm"

def layer_norm(x, g, b):
    x32 = x.astype(jnp.float32)
    mu = jnp.mean(x32, axis=-1, keepdims=True)
    var = jnp.mean(jnp.square(x32 - mu), axis=-1, keepdims=True)
    y = (x32 - mu) * lax.rsqrt(var + LN_EPS) * g.astype(jnp.float32) + b.astype(jnp.float32)
    return y.astype(x.dtype)

def rms_norm(x, g):
    x32 = x.astype(jnp.float32)
    y = x32 * lax.rsqrt(jnp.mean(jnp.square(x32), axis=-1, keepdims=True) + RMS_EPS)
    return (y * g.astype(jnp.float32)).astype(x.dtype)

def causal_dwconv(x, w):
    K = w.shape[0]
    S = x.shape[1]
    xp = jnp.pad(x, ((0, 0), (K - 1, 0), (0, 0)))
    y = w[K - 1] * x
    for k in range(K - 1):
        y = y + w[k] * xp[:, k:k + S]
    return y

def apply_rope(x, positions):
    D = x.shape[-1]
    inv_freq = ROPE_THETA ** (-jnp.arange(0, D, 2, dtype=jnp.float32) / D)
    ang = positions.astype(jnp.float32)[..., None] * inv_freq
    cos = jnp.cos(ang)[:, :, None, :]
    sin = jnp.sin(ang)[:, :, None, :]
    x32 = x.astype(jnp.float32)
    x1, x2 = x32[..., : D // 2], x32[..., D // 2:]
    out = jnp.concatenate([x1 * cos - x2 * sin, x1 * sin + x2 * cos], axis=-1)
    return out.astype(x.dtype)

def causal_block_attention(q, k, v):
    B, S, H, Dqk = q.shape
    Dv = v.shape[-1]
    nb = S // Q_BLOCK
    scale = Dqk ** -0.5
    qb = q.reshape(B, nb, Q_BLOCK, H, Dqk).transpose(1, 0, 2, 3, 4)
    key_pos = jnp.arange(S)

    def one_block(args):
        i, q_i = args
        s = jnp.einsum('bqhd,bkhd->bhqk', q_i, k,
                       preferred_element_type=jnp.float32) * scale
        q_pos = i * Q_BLOCK + jnp.arange(Q_BLOCK)
        mask = key_pos[None, :] <= q_pos[:, None]
        s = jnp.where(mask[None, None], s, -1e30)
        p = jax.nn.softmax(s, axis=-1)
        return jnp.einsum('bhqk,bkhd->bqhd', p.astype(v.dtype), v)

    out = lax.map(one_block, (jnp.arange(nb), qb))
    return out.transpose(1, 0, 2, 3, 4).reshape(B, S, H * Dv)

def hybrid_mixer(x, positions, w_in, q_norm_g, w_uq, kv_norm_g, w_ukv, conv_w, w_out):
    B, S, _ = x.shape
    h = jnp.einsum('bsd,de->bse', x, w_in)
    c_q, c_kv, k_r, gate_b, gate_c, x_c = jnp.split(h, IN_SPLITS, axis=-1)

    q = jnp.einsum('bsr,re->bse', rms_norm(c_q, q_norm_g), w_uq)
    q = q.reshape(B, S, MLA_HEADS, MLA_NOPE_DIM + MLA_ROPE_DIM)
    q_nope, q_rope = q[..., :MLA_NOPE_DIM], q[..., MLA_NOPE_DIM:]
    q_rope = apply_rope(q_rope, positions)
    kv = jnp.einsum('bsr,re->bse', rms_norm(c_kv, kv_norm_g), w_ukv)
    kv = kv.reshape(B, S, MLA_HEADS, MLA_NOPE_DIM + MLA_V_DIM)
    k_nope, v = kv[..., :MLA_NOPE_DIM], kv[..., MLA_NOPE_DIM:]
    k_rope = apply_rope(k_r[:, :, None, :], positions)
    q_full = jnp.concatenate([q_nope, q_rope], axis=-1)
    k_full = jnp.concatenate(
        [k_nope, jnp.broadcast_to(k_rope, (B, S, MLA_HEADS, MLA_ROPE_DIM))], axis=-1)
    attn_out = causal_block_attention(q_full, k_full, v)

    conv_out = gate_b * causal_dwconv(gate_c * x_c, conv_w)

    mixed = jnp.concatenate([attn_out, conv_out], axis=-1)
    return jnp.einsum('bse,ed->bsd', mixed, w_out)

def conv_ffn(x, w_gate_up, ffn_conv_w, w_down):
    gu = causal_dwconv(jnp.einsum('bsd,df->bsf', x, w_gate_up), ffn_conv_w)
    g, u = gu[..., :FFN_DIM], gu[..., FFN_DIM:]
    return jnp.einsum('bsf,fd->bsd', jax.nn.silu(g) * u, w_down)

def setup_inputs(seed: int = 0) -> dict:
    key = jax.random.key(seed)
    ks = jax.random.split(key, 18)
    f32 = jnp.float32

    def nrm(k, shape, scale):
        return jax.random.normal(k, shape, f32) * scale

    x = jax.random.normal(ks[0], (BATCH, SEQ, D_MODEL), f32)
    positions = jnp.broadcast_to(jnp.arange(SEQ, dtype=jnp.int32), (BATCH, SEQ))
    return {
        "x": x,
        "positions": positions,
        "w_in": nrm(ks[1], (DEPTH, D_MODEL, IN_PROJ_DIM), D_MODEL ** -0.5),
        "q_norm_g": 1.0 + nrm(ks[2], (DEPTH, Q_LORA_RANK), 0.02),
        "w_uq": nrm(ks[3], (DEPTH, Q_LORA_RANK, MLA_HEADS * (MLA_NOPE_DIM + MLA_ROPE_DIM)),
                    Q_LORA_RANK ** -0.5),
        "kv_norm_g": 1.0 + nrm(ks[4], (DEPTH, KV_LORA_RANK), 0.02),
        "w_ukv": nrm(ks[5], (DEPTH, KV_LORA_RANK, MLA_HEADS * (MLA_NOPE_DIM + MLA_V_DIM)),
                     KV_LORA_RANK ** -0.5),
        "conv_w": nrm(ks[6], (DEPTH, CONV_K, CONV_WIDTH), CONV_K ** -0.5),
        "w_out": nrm(ks[7], (DEPTH, D_MIX, D_MODEL), D_MIX ** -0.5) * DEEPNORM_BETA,
        "ln1_g": 1.0 + nrm(ks[8], (DEPTH, D_MODEL), 0.02),
        "ln1_b": nrm(ks[9], (DEPTH, D_MODEL), 0.02),
        "w_gate_up": nrm(ks[10], (DEPTH, D_MODEL, 2 * FFN_DIM), D_MODEL ** -0.5),
        "ffn_conv_w": nrm(ks[11], (DEPTH, FFN_CONV_K, 2 * FFN_DIM), FFN_CONV_K ** -0.5),
        "w_down": nrm(ks[12], (DEPTH, FFN_DIM, D_MODEL), FFN_DIM ** -0.5) * DEEPNORM_BETA,
        "ln2_g": 1.0 + nrm(ks[13], (DEPTH, D_MODEL), 0.02),
        "ln2_b": nrm(ks[14], (DEPTH, D_MODEL), 0.02),
    }

def reference(x, positions, w_in, q_norm_g, w_uq, kv_norm_g, w_ukv, conv_w, w_out,
              ln1_g, ln1_b, w_gate_up, ffn_conv_w, w_down, ln2_g, ln2_b):
    for l in range(DEPTH):
        mix = hybrid_mixer(x, positions, w_in[l], q_norm_g[l], w_uq[l], kv_norm_g[l],
                           w_ukv[l], conv_w[l], w_out[l])
        x = layer_norm(DEEPNORM_ALPHA * x + mix, ln1_g[l], ln1_b[l])
        ffn = conv_ffn(x, w_gate_up[l], ffn_conv_w[l], w_down[l])
        x = layer_norm(DEEPNORM_ALPHA * x + ffn, ln2_g[l], ln2_b[l])
    return x


_drawn_inputs = setup_inputs


def setup_inputs(seed=0):
    import zlib

    import numpy as np

    out = dict(_drawn_inputs(seed))
    spreads = {}
    factors = {'q_norm_g': 8.0,
     'kv_norm_g': 8.0,
     'ln1_g': 2.742,
     'ln2_g': 7.712,
     'ln2_b': 7.734,
     'ln1_b': 6.184}
    for name, (base, spread) in spreads.items():
        noise = np.random.default_rng([zlib.crc32(name.encode()), seed]).standard_normal(out[name].shape)
        drawn = base * np.exp(spread * noise) if base else spread * noise
        out[name] = __import__('jax').numpy.asarray(drawn.astype(out[name].dtype))
    for name, factor in factors.items():
        out[name] = (out[name] * factor).astype(out[name].dtype)
    return out
```

```python
import math
from contextlib import ExitStack

import numpy as np

import concourse.bass as bass
from concourse import mybir

ALU = mybir.AluOpType
ACT = mybir.ActivationFunctionType
AX_X = mybir.AxisListType.X
F32 = mybir.dt.float32
F32R = mybir.dt.float32r
I32 = mybir.dt.int32

P = 128
D_MODEL = 2048
SEQ = 512
HEADS = 8
NOPE = 128
ROPE = 64
HALF = ROPE // 2
VDIM = 128
Q_RANK = 512
KV_RANK = 256
CONV_WIDTH = D_MODEL - HEADS * VDIM
FFN = 5632
K = 3
LN_EPS = 1e-5
RMS_EPS = 1e-6
ALPHA = 2.0 ** 0.25
SCALE = float(NOPE + ROPE) ** -0.5
ROPE_THETA = 10000.0

KT = D_MODEL // P
TT = SEQ // P
NB = D_MODEL // 512
QT = Q_RANK // P
KVT = KV_RANK // P
FT = FFN // P
KV_COL = Q_RANK
KR_COL = Q_RANK + KV_RANK
B_COL = KR_COL + ROPE
C_COL = B_COL + CONV_WIDTH
X_COL = C_COL + CONV_WIDTH

PERIOD = 24
RAW = 4
SPLIT = 3
STAGE = 1024
S_ITER0 = 2 * (QT + KVT + 1)
S_HEADS = S_ITER0 + 16 - PERIOD
S_OUT_LAST = S_HEADS + PERIOD * (HEADS // 2)
S_CHUNK0 = S_OUT_LAST + 8
S_CHUNKS = S_CHUNK0 + 16 - PERIOD
CHUNKS = FT // 4
S_DOWN_LAST = S_CHUNKS + PERIOD * CHUNKS
S_END = S_DOWN_LAST + 8
N_ANGLE = 18
assert PERIOD % RAW == 0 and PERIOD % SPLIT == 0

IT0 = [dict(c=0, ukv=2, uq=3, x=4, b=6), dict(c=8, ukv=10, uq=11, x=12, b=14)]
ITN = [dict(c=0, ukv=2, uq=3, out=4, x=12, b=14), dict(c=16, ukv=18, uq=19, x=20, b=22)]

G1, B1, CW, QG, KVG = 0, KT, 2 * KT, 2 * KT + K * 8, 2 * KT + K * 8 + QT
N_ROWS = KVG + KVT


def shape_constants():
    c = np.zeros((P, 2 * P + 1), np.float32)
    c[:, :P] = np.eye(P)
    c[:, P:2 * P] = np.where(np.arange(P)[None, :] <= np.arange(P)[:, None], 0.0, -1e30)
    freq = np.float64(ROPE_THETA) ** (-np.arange(0, ROPE, 2) / ROPE)
    c[:, 2 * P] = np.tile(freq.astype(np.float32), P // HALF)
    return c


def two_pi_parts():
    parts, rest = [], 2.0 * math.pi
    for _ in range(3):
        unit = 2.0 ** (math.floor(math.log2(rest)) - 10)
        parts.append(math.floor(rest / unit) * unit)
        rest -= parts[-1]
    return parts + [rest]


def kind_of(number, looped):
    if looped and number < S_HEADS + PERIOD + SPLIT:
        local = (number - S_HEADS) % PERIOD
        return "plain" if local < SPLIT else next(
            (kind for at in ITN for kind in ("ukv", "uq") if at[kind] == local), "plain")
    if not looped and S_ITER0 - 2 <= number < S_ITER0:
        return "kr"
    if not looped and S_ITER0 <= number < S_ITER0 + 16:
        return next((kind for at in IT0 for kind in ("ukv", "uq") if at[kind] == number - S_ITER0), "plain")
    return "plain"


def hybrid_layer(nc, consts, x, positions, w_in, q_norm_g, w_uq, kv_norm_g, w_ukv, conv_w, w_out,
                 ln1_g, ln1_b, w_gate_up, ffn_conv_w, w_down, ln2_g, ln2_b, out):
    with ExitStack() as ctx:
        def sb(name, shape, dt=F32, stack=ctx):
            return stack.enter_context(nc.sbuf_tensor(name, shape, dt))

        def sem(name):
            return ctx.enter_context(nc.semaphore(name))

        const = sb("const", [P, 2 * P + 1])
        ident, mask, freq = const[:, 0:P], const[:, P:2 * P], const[:, 2 * P:2 * P + 1]
        ones = sb("ones", [P, P])
        eps = sb("eps", [P, 2])
        vec = sb("vec", [P, N_ROWS])
        fcw = sb("fcw", [P, K, 2 * FT])
        fw = sb("fw", [P, K, 2, 4])
        cw = sb("cw", [P, K, 2])
        stat = sb("stat", [P, TT, NB, 6])
        mv = sb("mv", [P, TT, 2])
        std = sb("std", [P, TT])
        rstd = sb("rstd", [P, TT])
        mx = sb("mx", [P, TT])
        nmx = sb("nmx", [P, TT])
        psum_p = sb("psum_p", [P, TT])
        rsum = sb("rsum", [P, TT])
        res = sb("res", [P, TT, D_MODEL])
        xh = sb("xh", [P, KT, SEQ], F32R)
        xl = sb("xl", [P, KT, SEQ], F32R)
        mh = sb("mh", [P, 4, SEQ], F32R)
        ml = sb("ml", [P, 4, SEQ], F32R)
        scr = sb("scr", [P, 6, SEQ])
        raw = sb("raw", [P, RAW, STAGE])
        wh = sb("wh", [P, SPLIT, STAGE], F32R)
        wl = sb("wl", [P, SPLIT, STAGE], F32R)
        with ExitStack() as heads_only:
            cqh = sb("cqh", [P, QT, SEQ], F32R, heads_only)
            cql = sb("cql", [P, QT, SEQ], F32R, heads_only)
            ckh = sb("ckh", [P, KVT, SEQ], F32R, heads_only)
            ckl = sb("ckl", [P, KVT, SEQ], F32R, heads_only)
            krh = sb("krh", [P, SEQ], F32R, heads_only)
            krl = sb("krl", [P, SEQ], F32R, heads_only)
            cs = sb("cs", [P, SEQ], F32, heads_only)
            att = sb("att", [P, 5 * SEQ], F32R, heads_only)
            vh = sb("vh", [P, TT, VDIM], F32R, heads_only)
            vl = sb("vl", [P, TT, VDIM], F32R, heads_only)
            sqs = sb("sqs", [P, 4, SEQ], F32, heads_only)
        with ExitStack() as ffn_only:
            gb = sb("gb", [P, 4, D_MODEL], F32, ffn_only)
        qnh, qnl, knh, knl, qp = (att[:, j * SEQ:(j + 1) * SEQ] for j in range(5))
        PT_OFF = [0, 512, 896, 1152, 1280]
        pth, ptl = att[:, 0:1280], att[:, 1280:2560]
        P_OFF = [0, 128, 384, 768, 1280]
        scr_flat = scr[:].rearrange("p a b -> p (a b)")
        prob = scr_flat[:, 0:1280]
        c_sb = scr_flat[:, 1280:1792]
        tmp_a = scr_flat[:, 1792:2304]
        tmp_b = scr_flat[:, 2304:2816]
        lat = [scr[:, j, :] for j in range(6)]
        rows = scr[:, 0, 0:P]
        frows = scr[:, 0, P:P + K * P].rearrange("p (k n) -> p k n", k=K)
        pos = scr[:, 1, :]
        ang, turns, turns_hi, turns_lo = (scr[:, j, :] for j in (2, 3, 4, 5))
        yg, yu, sg, a_f = (scr[:, j, :] for j in range(4))

        ps = [ctx.enter_context(nc.psum_tensor(f"bank{b}", [P, 512], F32)) for b in range(8)]
        B_LAT = [2, 3, 0, 1, 2, 3]
        B_KR, B_RMS = 4, [5, 6]
        B_C, B_PV, B_KN, B_V, B_QN, B_QR, B_X, B_B = 0, 1, 4, 5, 6, 7, 4, 5
        B_PT = [6, 7, 4]

        raw_landed = [sem(f"raw_landed{j}") for j in range(RAW)]
        x_landed = [sem(f"x_landed{t}") for t in range(TT)]
        (const_landed, rows_landed, pos_landed, gb_landed, out_written) = map(
            sem, ("const_landed", "rows_landed", "pos_landed", "gb_landed", "out_written"))
        (stage_used, rows_turned, x_turned, rms_sum, score_done, pt_done, pv_done, out_done, n_turned) = map(
            sem, ("stage_used", "rows_turned", "x_turned", "rms_sum", "score_done", "pt_done", "pv_done",
                  "out_done", "n_turned"))
        (split_hi, xh_ready, lat_squared, rms_root, lat_hi, cs_ready, kr_hi, c_copied, kn_hi, v_hi, qn_hi,
         qr_hi, exp_done, conv_hi, pt_hi, pv_hi, std_ready, n_hi, g_scaled, u_scaled, silu_done, act_hi) = map(
            sem, ("split_hi", "xh_ready", "lat_squared", "rms_root", "lat_hi", "cs_ready", "kr_hi",
                  "c_copied", "kn_hi", "v_hi", "qn_hi", "qr_hi", "exp_done", "conv_hi", "pt_hi", "pv_hi",
                  "std_ready", "n_hi", "g_scaled", "u_scaled", "silu_done", "act_hi"))
        (split_lo, set_up, angle_step, vec_ready, xl_ready, sq_added, rms_inv, lat_normed, lat_lo,
         kr_prod, kr_rot, kr_lo) = map(
            sem, ("split_lo", "set_up", "angle_step", "vec_ready", "xl_ready", "sq_added", "rms_inv",
                  "lat_normed", "lat_lo", "kr_prod", "kr_rot", "kr_lo"))
        (cw_ready, kn_lo, v_lo, qn_lo, qr_prod, qr_rot, qr_lo, x_used, conv_tap, b_used, conv_lo, masked,
         max_taken, max_ready, sum_inv, p_ready, pt_lo, pv_lo, out_added) = map(
            sem, ("cw_ready", "kn_lo", "v_lo", "qn_lo", "qr_prod", "qr_rot", "qr_lo", "x_used", "conv_tap",
                  "b_used", "conv_lo", "masked", "max_taken", "max_ready", "sum_inv", "p_ready", "pt_lo",
                  "pv_lo", "out_added"))
        (stats_taken, var_ready, rstd_ready, normed, n_full, n_lo, fw_ready, g_tap, g_conv, u_tap, u_conv,
         act_full, act_lo, ln2_step, out_ready) = map(
            sem, ("stats_taken", "var_ready", "rstd_ready", "normed", "n_full", "n_lo", "fw_ready", "g_tap",
                  "g_conv", "u_tap", "u_conv", "act_full", "act_lo", "ln2_step", "out_ready"))
        x_scaled, res_step, res_ready = sem("x_scaled"), sem("res_step"), sem("res_ready")

        def ahead(stage, n):
            return (stage[0] + n, stage[1])

        def wait_stage(eng, s, stage, back=0):
            number, i = stage
            if number + 1 - back > 0:
                eng.wait_ge(s, number + 1 - back + PERIOD * i)

        def pieces(stage):
            number, i = stage
            r, h, low = raw[:, number % RAW, :], wh[:, number % SPLIT, :], wl[:, number % SPLIT, :]
            kind = kind_of(number, not isinstance(i, int))
            if kind == "plain":
                return [(r, h, low)]
            if kind == "ukv":
                return [(r[:, 0:512], h[:, 0:512], low[:, 0:512])]
            lead, k = (NOPE, QT) if kind == "uq" else (0, 8)
            width = lead + ROPE
            r3 = r[:, 0:k * width].rearrange("p (k n) -> p k n", n=width)
            h3, l3 = (v[:, 0:k * (width + ROPE)].rearrange("p (k n) -> p k n", n=width + ROPE) for v in (h, low))
            return [(r3[:, :, a:b], h3[:, :, to:to + b - a], l3[:, :, to:to + b - a])
                    for a, b, to in ((0, width, 0), (lead + HALF, width, width),
                                     (lead, lead + HALF, width + HALF))]

        def split_high(stage):
            number, i = stage
            if isinstance(i, int) and number >= S_END:
                return
            act = nc.scalar
            act.wait_ge(raw_landed[number % RAW], 16 * (number // RAW + 1) + 16 * (PERIOD // RAW) * i)
            wait_stage(act, stage_used, stage, back=SPLIT)
            for r, h, _ in pieces(stage):
                last = act.copy(h, r)
            last.then_inc(split_hi, 1)

        def split_low(stage):
            number, i = stage
            if isinstance(i, int) and number >= S_END:
                return
            dve = nc.vector
            wait_stage(dve, split_hi, stage)
            for r, h, low in pieces(stage):
                last = dve.tensor_tensor(low, r, h.bitcast(F32), ALU.subtract)
            last.then_inc(split_lo, 1)

        block = ctx.enter_context(nc.Block())

        @block.sync
        def _(sp):
            w_in_t = w_in[0].rearrange("(h k p) n -> h p k n", h=2, p=P)
            w_uq_t = w_uq[0].rearrange("(k p) n -> p k n", p=P)
            w_ukv_t = w_ukv[0].rearrange("(k p) n -> p k n", p=P)
            w_out_t = w_out[0].rearrange("(g h p) n -> p g h n", g=2, p=P)
            w_gu_t = w_gate_up[0].rearrange("(h k p) n -> h p k n", h=2, p=P)
            w_down_t = w_down[0].rearrange("(k p) n -> p k n", p=P)

            def load(stage, rows_, start, count, source):
                number, i = stage
                dst = raw[:, number % RAW, 0:rows_ * count].rearrange("p (k n) -> p k n", n=count)
                at = start if isinstance(start, int) else sp.snap(start)
                wait_stage(sp, split_lo, stage, back=RAW)
                sp.dma_start(dst, source(at)).then_inc(raw_landed[number % RAW], 16)

            def load_in(stage, column, width=P):
                for h in range(2):
                    load(ahead(stage, h), 8, column, width, lambda at: w_in_t[h][:, :, bass.ds(at, width)])

            def load_out(stage, i):
                for n in range(NB):
                    for j in range(2):
                        load(ahead(stage, 2 * n + j), 2, 2 * i + j, 512, lambda at: w_out_t[
                            :, :, bass.ds(at, 1), n * 512:(n + 1) * 512].rearrange("p g h n -> p (g h) n"))

            def load_down(stage, c):
                for n in range(NB):
                    for j in range(2):
                        load(ahead(stage, 2 * n + j), 2, 4 * c + 2 * j, 512, lambda at: w_down_t[
                            :, bass.ds(at, 2), n * 512:(n + 1) * 512])

            def load_heads(base, i, table):
                for hh, at in enumerate(table):
                    head = 2 * i + hh
                    load_in(ahead(base, at["c"]), C_COL + P * head)
                    load(ahead(base, at["ukv"]), KVT, 256 * head, 256, lambda a: w_ukv_t[:, :, bass.ds(a, 256)])
                    load(ahead(base, at["uq"]), QT, 192 * head, 192, lambda a: w_uq_t[:, :, bass.ds(a, 192)])
                    if "out" in at:
                        load_out(ahead(base, at["out"]), i - 1)
                    load_in(ahead(base, at["x"]), X_COL + P * head)
                    load_in(ahead(base, at["b"]), B_COL + P * head)

            def load_pair(stage, tile):
                for j in range(2):
                    for h in range(2):
                        load(ahead(stage, 2 * j + h), 8, j * FFN + P * tile, P,
                             lambda at: w_gu_t[h][:, :, bass.ds(at, P)])

            for t in range(TT):
                sp.dma_start(res[:, t, :], x[0, t * P:(t + 1) * P, :]).then_inc(x_landed[t], 16)
            load_in((0, 0), KV_COL)
            load_in((2, 0), KV_COL + P)
            for j in range(QT):
                load_in((4 + 2 * j, 0), j * P)
            load_in((12, 0), KR_COL, ROPE)
            load_heads((S_ITER0, 0), 0, IT0)
            with sp.Fori(1, HEADS // 2) as i:
                load_heads((S_HEADS, i), i, ITN)
            load_out((S_OUT_LAST, 0), HEADS // 2 - 1)
            for q in range(3):
                load_pair((S_CHUNK0 + 4 * q, 0), q)
            sp.wait_ge(pv_done, HEADS)
            for j, v in enumerate((ln1_g, ln1_b, ln2_g, ln2_b)):
                sp.dma_start(gb[:, j, :], v[0].partition_broadcast(P)).then_inc(gb_landed, 16)
            load_pair((S_CHUNK0 + 12, 0), 3)
            with sp.Fori(1, CHUNKS) as c:
                load_pair((S_CHUNKS, c), 4 * c)
                load_down((S_CHUNKS + 4, c), c - 1)
                for q in range(1, 4):
                    load_pair((S_CHUNKS + 8 + 4 * q, c), 4 * c + q)
            load_down((S_DOWN_LAST, 0), CHUNKS - 1)
            for t in range(TT):
                sp.wait_ge(out_ready, t + 1)
                sp.dma_start(out[0, t * P:(t + 1) * P, :], res[:, t, :]).then_inc(out_written, 16)
            sp.wait_ge(out_written, 16 * TT)

        @block.tensor
        def _(pe):
            def pieces3(stage, width):
                number = stage[0]
                return [w[:, number % SPLIT, 0:STAGE // width * width].rearrange("p (k n) -> p k n", n=width)
                        for w in (wh, wl)]

            def products(dst, pairs):
                for n, (sh, sl, vh_, vl_) in enumerate(pairs):
                    pe.matmul(dst, sh, vh_, start=(n == 0), stop=False)
                    pe.matmul(dst, sl, vh_, start=False, stop=False)
                    last = pe.matmul(dst, sh, vl_, start=False, stop=(n == len(pairs) - 1))
                return last

            def project(stage, bank, need=None):
                for h in range(2):
                    st = ahead(stage, h)
                    wait_stage(pe, split_lo, st)
                    w3h, w3l = pieces3(st, P)
                    for k in range(8):
                        kk = 8 * h + k
                        if need is not None:
                            pe.wait_ge(need, kk + 1)
                        for j, (w, v) in enumerate(((w3h, xh), (w3l, xh), (w3h, xl))):
                            last = pe.matmul(ps[bank][:], w[:, k, :], v[:, kk, :],
                                             start=(kk == 0 and j == 0), stop=(kk == KT - 1 and j == 2))
                    last.then_inc(stage_used, 1)

            def project_out(stage, m, first):
                for n in range(NB):
                    for j in range(2):
                        st = ahead(stage, 2 * n + j)
                        wait_stage(pe, split_lo, st)
                        w3h, w3l = pieces3(st, 512)
                        if n == 0:
                            first(j)
                        for t in range(TT):
                            if j == 0 and n > 0:
                                pe.wait_ge(out_added, 16 * m + 4 * (n - 1) + t + 1)
                            tok = slice(t * P, (t + 1) * P)
                            for k in range(2):
                                slot = 2 * j + k
                                for q, (v, w) in enumerate(((mh, w3h), (ml, w3h), (mh, w3l))):
                                    last = pe.matmul(ps[t][:], v[:, slot, tok], w[:, k, :],
                                                     start=(slot == 0 and q == 0),
                                                     stop=(slot == 3 and q == 2))
                            if j == 1 and t < TT - 1:
                                last.then_inc(out_done, 1)
                        last.then_inc(stage_used, 1)

            pe.wait_ge(const_landed, 16)
            pe.wait_ge(rows_landed, 16 * 6)
            pe.transpose(ps[0][:, 0:N_ROWS], rows[0:N_ROWS, :], ident[0:N_ROWS, 0:N_ROWS]).then_inc(rows_turned, 1)
            for k in range(K):
                last = pe.transpose(ps[1][:, k * 2 * FT:(k + 1) * 2 * FT], frows[0:2 * FT, k, :],
                                    ident[0:2 * FT, 0:2 * FT])
            last.then_inc(rows_turned, 1)
            for k in range(KT):
                for t in range(TT):
                    if k == 0:
                        pe.wait_ge(x_landed[t], 16)
                    if k >= 4 and t == 0:
                        pe.wait_ge(xl_ready, k - 3)
                    last = pe.transpose(ps[4 + k % 4][:, t * P:(t + 1) * P], res[:, t, k * P:(k + 1) * P], ident)
                last.then_inc(x_turned, 1)
            for j in range(6):
                if j == 2:
                    pe.wait_ge(vec_ready, 2)
                if j >= 4:
                    pe.wait_ge(lat_squared, j - 3)
                project((2 * j, 0), B_LAT[j], xl_ready if j == 0 else None)
                if j == 2:
                    pe.wait_ge(sq_added, 1)
                    pe.matmul(ps[B_RMS[0]][:], ones[:], sqs[:, 2, :], start=True, stop=True).then_inc(rms_sum, 1)
            for h in range(2):
                wait_stage(pe, split_lo, (12 + h, 0))
                w3h, w3l = pieces3((12 + h, 0), P)
                for k in range(8):
                    kk = 8 * h + k
                    for j, (w, v) in enumerate(((w3h, xh), (w3l, xh), (w3h, xl))):
                        last = pe.matmul(ps[B_KR][:], w[:, k, :], v[:, kk, :],
                                         start=(kk == 0 and j == 0), stop=(kk == KT - 1 and j == 2))
                last.then_inc(stage_used, 1)
                if h == 0:
                    pe.wait_ge(sq_added, 4)
                    pe.matmul(ps[B_RMS[1]][:], ones[:], sqs[:, 3, :], start=True, stop=True).then_inc(rms_sum, 1)

            def values(head):
                n = 0
                for j in range(TT):
                    pe.wait_ge(pt_lo, 3 * head + min(j, 2) + 1)
                    cols = slice(PT_OFF[j], PT_OFF[j + 1])
                    for v, p in ((vh, pth), (vl, pth), (vh, ptl)):
                        last = pe.matmul(ps[B_PV][:, j * P:512], v[:, j, :], p[:, cols],
                                         start=(n == 0), stop=(n == 11))
                        n += 1
                last.then_inc(pv_done, 1)

            def heads(base, i, table, first):
                for hh, at in enumerate(table):
                    head = 2 * i + hh
                    project(ahead(base, at["c"]), B_C)
                    if not (first and hh == 0):
                        values(head - 1)
                    st = ahead(base, at["ukv"])
                    wait_stage(pe, split_lo, st)
                    if first and hh == 0:
                        pe.wait_ge(lat_lo, KVT)
                        pe.wait_ge(kr_prod, 2)
                    else:
                        pe.wait_ge(b_used, head)
                    w3h, w3l = pieces3(st, 256)
                    products(ps[B_KN][:], [(w3h[:, k, 0:NOPE], w3l[:, k, 0:NOPE], ckh[:, k, :], ckl[:, k, :])
                                           for k in range(KVT)])
                    for t in range(TT):
                        tok = slice(t * P, (t + 1) * P)
                        last = products(ps[B_V][:, tok], [
                            (ckh[:, k, tok], ckl[:, k, tok], w3h[:, k, NOPE:], w3l[:, k, NOPE:]) for k in range(KVT)])
                    last.then_inc(stage_used, 1)
                    st = ahead(base, at["uq"])
                    wait_stage(pe, split_lo, st)
                    if first and hh == 0:
                        pe.wait_ge(lat_lo, KVT + QT)
                    w3h, w3l = pieces3(st, 256)
                    for bank, a in ((B_QN, 0), (B_QR, NOPE)):
                        last = products(ps[bank][:], [(w3h[:, k, a:a + P], w3l[:, k, a:a + P], cqh[:, k, :], cql[:, k, :])
                                                      for k in range(QT)])
                    last.then_inc(stage_used, 1)
                    if "out" in at:
                        def ready(j):
                            if j == 0:
                                pe.wait_ge(c_copied, head + 1)
                                pe.wait_ge(pv_lo, 2 * i)
                                pe.wait_ge(conv_lo, 2 * i)
                        project_out(ahead(base, at["out"]), i - 1, ready)
                    pe.wait_ge(kn_lo, head + 1)
                    project(ahead(base, at["x"]), B_X)
                    pe.wait_ge(qn_lo, head + 1)
                    pe.wait_ge(qr_lo, head + 1)
                    if first and hh == 0:
                        pe.wait_ge(kr_lo, 1)
                    if "out" in at:
                        pe.wait_ge(out_added, 16 * i)
                    else:
                        pe.wait_ge(c_copied, head + 1)
                        if not (first and hh == 0):
                            pe.wait_ge(pv_lo, head)
                    for j in range(TT):
                        tok, keys = slice(j * P, (j + 1) * P), slice(0, (j + 1) * P)
                        for n, (a, b) in enumerate(((qnh, knh), (qnl, knh), (qnh, knl), (qp, krh), (qp, krl))):
                            last = pe.matmul(ps[j][:, keys], a[:, tok], b[:, keys], start=(n == 0), stop=(n == 4))
                        last.then_inc(score_done, 1)
                    pe.wait_ge(v_lo, head + 1)
                    project(ahead(base, at["b"]), B_B)
                    pe.wait_ge(x_used, head + 1)
                    pe.wait_ge(p_ready, 4 * head + 4)
                    for n, tiles in enumerate(((0,), (1,), (2, 3))):
                        for j in tiles:
                            for q in range(j, TT):
                                to = PT_OFF[j] - PT_OFF[tiles[0]] + (q - j) * P
                                last = pe.transpose(ps[B_PT[n]][:, to:to + P],
                                                    prob[:, P_OFF[q] + j * P:P_OFF[q] + (j + 1) * P], ident)
                        last.then_inc(pt_done, 1)

            heads((S_ITER0, 0), 0, IT0, True)
            with pe.Fori(1, HEADS // 2) as i:
                heads((S_HEADS, i), i, ITN, False)
            values(HEADS - 1)

            def ready(j):
                if j == 0:
                    pe.wait_ge(pv_lo, HEADS)
                    pe.wait_ge(conv_lo, HEADS)
            project_out((S_OUT_LAST, 0), HEADS // 2 - 1, ready)

            for k in range(KT):
                pe.wait_ge(normed, 4 * (k // 4) + 4)
                if k >= 4:
                    pe.wait_ge(n_full, k - 3)
                for t in range(TT):
                    last = pe.transpose(ps[4 + k % 4][:, t * P:(t + 1) * P], res[:, t, k * P:(k + 1) * P], ident)
                last.then_inc(n_turned, 1)

            def pair(stage, q, c, first):
                for j, free in enumerate((g_conv, u_conv)):
                    if first and q < 2:
                        pe.wait_ge(n_full, KT)
                    else:
                        pe.wait_ge(free, 4 * c + q - 1)
                    project(ahead(stage, 2 * j), 4 + 2 * (q % 2) + j, n_lo if first and q == 0 and j == 0 else None)

            def down(stage, c):
                def ready(j):
                    pe.wait_ge(out_added, 16 * (c + HEADS // 2))
                    pe.wait_ge(act_lo, 4 * c + 2 * j + 2)
                project_out(stage, c + HEADS // 2, ready)

            for q in range(4):
                pair((S_CHUNK0 + 4 * q, 0), q, 0, True)
            with pe.Fori(1, CHUNKS) as c:
                pair((S_CHUNKS, c), 0, c, False)
                down((S_CHUNKS + 4, c), c - 1)
                for q in range(1, 4):
                    pair((S_CHUNKS + 8 + 4 * q, c), q, c, False)
            down((S_DOWN_LAST, 0), CHUNKS - 1)

        @block.scalar
        def _(act):
            def after(stage):
                split_high(ahead(stage, SPLIT))

            act.dma_start(const[:], consts).then_inc(const_landed, 16)
            for at, v in ((G1, ln1_g[0].rearrange("(k p) -> k p", p=P)), (B1, ln1_b[0].rearrange("(k p) -> k p", p=P)),
                          (CW, conv_w[0].rearrange("k (h p) -> (k h) p", p=P)),
                          (QG, q_norm_g[0].rearrange("(k p) -> k p", p=P)),
                          (KVG, kv_norm_g[0].rearrange("(k p) -> k p", p=P))):
                act.dma_start(rows[at:at + v.shape[0], :], v).then_inc(rows_landed, 16)
            act.dma_start(frows[0:2 * FT], ffn_conv_w[0].rearrange("k (r p) -> r k p", p=P)).then_inc(rows_landed, 16)
            act.dma_start(pos.bitcast(I32), positions[0].partition_broadcast(P)).then_inc(pos_landed, 16)
            for s in range(SPLIT):
                split_high((s, 0))
            act.wait_ge(angle_step, N_ANGLE)
            act.activation(cs[:], ang, ACT.Sin).then_inc(cs_ready, 1)
            for k in range(KT):
                act.wait_ge(x_turned, k + 1)
                act.copy(xh[:, k, :], ps[4 + k % 4][:]).then_inc(xh_ready, 1)

            def latent(j):
                act.copy(lat[j], ps[B_LAT[j]][:])
                if j >= 2:
                    act.wait_ge(sq_added, 1 if j < 4 else 2)
                act.activation(sqs[:, j % 2, :], ps[B_LAT[j]][:], ACT.Square).then_inc(lat_squared, 1)

            def root(n, rank, dst):
                act.wait_ge(rms_sum, n + 1)
                act.activation(dst, ps[B_RMS[n]][:], ACT.Sqrt, bias=eps[:, 1:2], scale=1.0 / rank).then_inc(rms_root, 1)

            for s in range(2 * (KVT + QT)):
                wait_stage(act, stage_used, (s, 0))
                if s % 2 == 1:
                    latent(s // 2)
                after((s, 0))
                if s == 5:
                    root(0, KV_RANK, sqs[:, 2, :])
                    for k in range(KVT):
                        act.wait_ge(lat_normed, k + 1)
                        act.copy(ckh[:, k, :], lat[k]).then_inc(lat_hi, 1)
            after((12, 0))
            root(1, Q_RANK, sqs[:, 3, :])
            for k in range(QT):
                act.wait_ge(lat_normed, KVT + k + 1)
                act.copy(cqh[:, k, :], lat[KVT + k]).then_inc(lat_hi, 1)
            after((13, 0))
            act.wait_ge(kr_rot, 1)
            act.copy(krh[0:ROPE, :], sqs[0:ROPE, 0, :])
            act.copy(krh[ROPE:P, :], sqs[0:ROPE, 0, :]).then_inc(kr_hi, 1)

            def values_high(head, slot):
                act.wait_ge(pv_done, head + 1)
                act.copy(mh[:, slot, :], ps[B_PV][:]).then_inc(pv_hi, 1)

            def heads(base, i, table, first):
                for hh, at in enumerate(table):
                    head = 2 * i + hh

                    def st(name, n=0):
                        return ahead(base, at[name] + n)
                    after(st("c"))
                    wait_stage(act, stage_used, st("c", 1))
                    act.copy(c_sb, ps[B_C][:]).then_inc(c_copied, 1)
                    after(st("c", 1))
                    if not (first and hh == 0):
                        values_high(head - 1, 2 * (1 - hh))
                    wait_stage(act, stage_used, st("ukv"))
                    act.copy(knh, ps[B_KN][:]).then_inc(kn_hi, 1)
                    act.copy(vh[:].rearrange("p t n -> p (t n)"), ps[B_V][:]).then_inc(v_hi, 1)
                    after(st("ukv"))
                    wait_stage(act, stage_used, st("uq"))
                    act.copy(qnh, ps[B_QN][:]).then_inc(qn_hi, 1)
                    act.wait_ge(qr_rot, head + 1)
                    act.copy(qp[0:ROPE, :], tmp_a[0:ROPE, :]).then_inc(qr_hi, 1)
                    after(st("uq"))
                    if "out" in at:
                        for n in range(2 * NB):
                            after(st("out", n))
                    after(st("x"))
                    after(st("x", 1))
                    act.wait_ge(max_ready, head + 1)
                    for j in range(TT):
                        act.activation(prob[:, P_OFF[j]:P_OFF[j + 1]], ps[j][:, 0:(j + 1) * P], ACT.Exp,
                                       bias=nmx[:, j:j + 1], scale=SCALE,
                                       accum_out=psum_p[:, j:j + 1]).then_inc(exp_done, 1)
                    after(st("b"))
                    act.wait_ge(b_used, head + 1)
                    act.copy(mh[:, 2 * hh + 1, :], tmp_a).then_inc(conv_hi, 1)
                    after(st("b", 1))
                    for n in range(3):
                        act.wait_ge(pt_done, 3 * head + n + 1)
                        a, b = PT_OFF[n], PT_OFF[n + 1 if n < 2 else 4]
                        act.copy(pth[:, a:b], ps[B_PT[n]][:, 0:b - a]).then_inc(pt_hi, 1)

            heads((S_ITER0, 0), 0, IT0, True)
            with act.Fori(1, HEADS // 2) as i:
                heads((S_HEADS, i), i, ITN, False)
            values_high(HEADS - 1, 2)
            for n in range(2 * NB):
                after((S_OUT_LAST + n, 0))

            act.wait_ge(var_ready, TT)
            act.activation(std[:], mv[:, :, 1], ACT.Sqrt, bias=eps[:, 0:1]).then_inc(std_ready, 1)
            for k in range(KT):
                act.wait_ge(n_full, k + 1)
                act.copy(xh[:, k, :], scr[:, 4 + k % 2, :]).then_inc(n_hi, 1)

            def gates(stage, q, c):
                after(stage)
                wait_stage(act, stage_used, ahead(stage, 1))
                act.wait_ge(fw_ready, c + 1)
                act.activation(yg, ps[4 + 2 * (q % 2)][:], ACT.Copy, scale=fw[:, K - 1, 0, q:q + 1]).then_inc(g_scaled, 1)
                after(ahead(stage, 1))
                after(ahead(stage, 2))
                wait_stage(act, stage_used, ahead(stage, 3))
                act.activation(yu, ps[5 + 2 * (q % 2)][:], ACT.Copy, scale=fw[:, K - 1, 1, q:q + 1]).then_inc(u_scaled, 1)
                act.wait_ge(g_conv, 4 * c + q + 1)
                act.activation(sg, yg, ACT.Silu).then_inc(silu_done, 1)
                after(ahead(stage, 3))

            def act_high(q, c):
                act.wait_ge(act_full, 4 * c + q + 1)
                act.copy(mh[:, q, :], a_f).then_inc(act_hi, 1)

            for q in range(4):
                gates((S_CHUNK0 + 4 * q, 0), q, 0)
                act_high(q, 0)
            with act.Fori(1, CHUNKS) as c:
                gates((S_CHUNKS, c), 0, c)
                for n in range(2 * NB):
                    after((S_CHUNKS + 4 + n, c))
                act_high(0, c)
                for q in range(1, 4):
                    gates((S_CHUNKS + 8 + 4 * q, c), q, c)
                    act_high(q, c)
            for n in range(2 * NB):
                after((S_DOWN_LAST + n, 0))
            act.wait_ge(var_ready, 2 * TT)
            act.activation(std[:], mv[:, :, 1], ACT.Sqrt, bias=eps[:, 0:1]).then_inc(std_ready, 1)

        @block.vector
        def _(dve):
            def after(stage):
                split_low(ahead(stage, SPLIT))

            dve.memset(eps[:, 0:1], LN_EPS)
            dve.memset(eps[:, 1:2], RMS_EPS)
            dve.memset(ones[:], 1.0)
            dve.memset(krl[ROPE:P, :].bitcast(F32), 0.0).then_inc(set_up, 1)
            for s in range(SPLIT):
                split_low((s, 0))

            count = [0]

            def step(ins):
                count[0] += 1
                ins.then_inc(angle_step, 1)
                dve.wait_ge(angle_step, count[0])

            dve.wait_ge(pos_landed, 16)
            dve.wait_ge(const_landed, 16)
            step(dve.tensor_copy(ang, pos.bitcast(I32)))
            step(dve.tensor_scalar(ang, ang, freq, None, ALU.mult))
            step(dve.tensor_scalar(turns, ang, 1.0 / (2.0 * math.pi), 1.5 * 2.0 ** 23, ALU.mult, ALU.add))
            step(dve.tensor_scalar(turns, turns, -1.5 * 2.0 ** 23, None, ALU.add))
            step(dve.tensor_scalar(turns_hi, turns, 1.5 * 2.0 ** 34, None, ALU.add))
            step(dve.tensor_scalar(turns_hi, turns_hi, -1.5 * 2.0 ** 34, None, ALU.add))
            step(dve.tensor_tensor(turns_lo, turns, turns_hi, ALU.subtract))
            parts = two_pi_parts()
            for part, counts in ((parts[0], (turns_hi, turns_lo)), (parts[1], (turns_hi, turns_lo)),
                                 (parts[2], (turns_hi, turns_lo)), (parts[3], (turns,))):
                for n in counts:
                    step(dve.scalar_tensor_tensor(ang, n, -part, ang, ALU.mult, ALU.add))
            step(dve.tensor_scalar(ang, ang, math.pi, -math.pi, ALU.min, ALU.max))
            step(dve.scalar_tensor_tensor(ang[0:ROPE, :], ang[0:ROPE, :], -1.0, ang[0:ROPE, :], ALU.mult, ALU.max))
            step(dve.tensor_scalar(ang[0:ROPE, :], ang[0:ROPE, :], -1.0, math.pi / 2, ALU.mult, ALU.add))
            step(dve.tensor_scalar(ang[ROPE:ROPE + HALF, :], ang[ROPE:ROPE + HALF, :], -1.0, None, ALU.mult))
            assert count[0] == N_ANGLE, count

            dve.wait_ge(rows_turned, 1)
            dve.tensor_copy(vec[:], ps[0][:, 0:N_ROWS]).then_inc(vec_ready, 1)
            dve.wait_ge(rows_turned, 2)
            dve.tensor_copy(fcw[:].rearrange("p k n -> p (k n)"), ps[1][:, 0:K * 2 * FT]).then_inc(vec_ready, 1)
            for k in range(KT):
                dve.wait_ge(xh_ready, k + 1)
                dve.tensor_tensor(xl[:, k, :], ps[4 + k % 4][:], xh[:, k, :].bitcast(F32),
                                  ALU.subtract).then_inc(xl_ready, 1)

            def norm_latents(n, first, tiles, gain, high, low):
                inv = sqs[:, 2 + n, :]
                dve.wait_ge(rms_root, n + 1)
                dve.reciprocal(inv, inv).then_inc(rms_inv, 1)
                dve.wait_ge(rms_inv, n + 1)
                dve.wait_ge(vec_ready, 1)
                for k in range(tiles):
                    dve.scalar_tensor_tensor(lat[first + k], lat[first + k], vec[:, gain + k:gain + k + 1], inv,
                                             ALU.mult, ALU.mult).then_inc(lat_normed, 1)
                for k in range(tiles):
                    dve.wait_ge(lat_hi, first + k + 1)
                    dve.tensor_tensor(low[:, k, :], lat[first + k], high[:, k, :].bitcast(F32),
                                      ALU.subtract).then_inc(lat_lo, 1)

            for s in range(2 * (KVT + QT)):
                after((s, 0))
                if s % 2 == 1:
                    j = s // 2
                    dve.wait_ge(lat_squared, j + 1)
                    if j == 1:
                        dve.tensor_tensor(sqs[:, 2, :], sqs[:, 0, :], sqs[:, 1, :], ALU.add).then_inc(sq_added, 1)
                    if j == 3:
                        dve.tensor_tensor(sqs[:, 3, :], sqs[:, 0, :], sqs[:, 1, :], ALU.add).then_inc(sq_added, 1)
                    if j > 3:
                        dve.wait_ge(sq_added, j - 2)
                        dve.tensor_tensor(sqs[:, 3, :], sqs[:, 3, :], sqs[:, j % 2, :], ALU.add).then_inc(sq_added, 1)
                if s == 5:
                    norm_latents(0, 0, KVT, KVG, ckh, ckl)
            after((12, 0))
            norm_latents(1, KVT, QT, QG, cqh, cql)
            after((13, 0))

            def rotate(bank, dst, spare, products_, rotated):
                dve.tensor_tensor(dst[0:ROPE, :], ps[bank][0:ROPE, :], cs[0:ROPE, :], ALU.mult).then_inc(products_[0], 1)
                dve.tensor_tensor(spare[0:ROPE, :], ps[bank][ROPE:P, :], cs[ROPE:P, :], ALU.mult).then_inc(products_[0], 1)
                dve.wait_ge(*products_)
                dve.tensor_tensor(dst[0:ROPE, :], dst[0:ROPE, :], spare[0:ROPE, :], ALU.add).then_inc(rotated, 1)

            dve.wait_ge(cs_ready, 1)
            wait_stage(dve, stage_used, (13, 0))
            rotate(B_KR, sqs[:, 0, :], sqs[:, 1, :], (kr_prod, 2), kr_rot)
            dve.wait_ge(kr_hi, 1)
            dve.tensor_tensor(krl[0:ROPE, :], sqs[0:ROPE, 0, :], krh[0:ROPE, :].bitcast(F32),
                              ALU.subtract).then_inc(kr_lo, 1)

            def low_of(dst, full, high, have, n, s):
                dve.wait_ge(have, n)
                dve.tensor_tensor(dst, full, high.bitcast(F32), ALU.subtract).then_inc(s, 1)

            def add_out(stage, m, stats):
                for n in range(NB):
                    after(ahead(stage, 2 * n))
                    for t in range(TT):
                        if t < TT - 1:
                            dve.wait_ge(out_done, 12 * m + 3 * n + t + 1)
                        else:
                            wait_stage(dve, stage_used, ahead(stage, 2 * n + 1))
                        block_ = res[:, t, n * 512:(n + 1) * 512]
                        dve.tensor_tensor(block_, block_, ps[t][:], ALU.add).then_inc(out_added, 1)
                    if stats is not None:
                        for t in range(TT):
                            dve.wait_ge(out_added, 16 * m + 4 * n + t + 1)
                            dve.bn_stats(stat[:, t, n, :], res[:, t, n * 512:(n + 1) * 512]).then_inc(stats_taken, 1)
                    after(ahead(stage, 2 * n + 1))

            def statistics(n):
                for t in range(TT):
                    dve.wait_ge(stats_taken, 16 * n + 12 + t + 1)
                    dve.bn_aggr(mv[:, t, :], stat[:, t, :, :].rearrange("p n s -> p (n s)")).then_inc(var_ready, 1)
                dve.wait_ge(std_ready, n + 1)
                dve.reciprocal(rstd[:], std[:]).then_inc(rstd_ready, 1)
                dve.wait_ge(rstd_ready, n + 1)

            def heads(base, i, table, first):
                dve.tensor_copy(cw[:], vec[:, CW:CW + K * 8].rearrange("p (k h) -> p k h", k=K)[
                    :, :, bass.ds(2 * i, 2)]).then_inc(cw_ready, 1)
                for hh, at in enumerate(table):
                    head = 2 * i + hh

                    def st(name, n=0):
                        return ahead(base, at[name] + n)
                    after(st("c"))
                    after(st("c", 1))
                    if not (first and hh == 0):
                        low_of(ml[:, 2 * (1 - hh), :], ps[B_PV][:], mh[:, 2 * (1 - hh), :], pv_hi, head, pv_lo)
                    low_of(knl, ps[B_KN][:], knh, kn_hi, head + 1, kn_lo)
                    low_of(vl[:].rearrange("p t n -> p (t n)"), ps[B_V][:], vh[:].rearrange("p t n -> p (t n)"),
                           v_hi, head + 1, v_lo)
                    after(st("ukv"))
                    wait_stage(dve, stage_used, st("uq"))
                    rotate(B_QR, tmp_a, tmp_b, (qr_prod, 2 * head + 2), qr_rot)
                    low_of(qnl, ps[B_QN][:], qnh, qn_hi, head + 1, qn_lo)
                    low_of(qp[ROPE:P, :], tmp_a[0:ROPE, :], qp[0:ROPE, :], qr_hi, head + 1, qr_lo)
                    after(st("uq"))
                    if "out" in at:
                        dve.wait_ge(x_scaled, TT)
                        add_out(st("out"), i - 1, None)
                    after(st("x"))
                    wait_stage(dve, stage_used, st("x", 1))
                    dve.wait_ge(c_copied, head + 1)
                    dve.wait_ge(qr_lo, head + 1)
                    dve.tensor_tensor(tmp_a, ps[B_X][:], c_sb, ALU.mult).then_inc(x_used, 1)
                    dve.wait_ge(x_used, head + 1)
                    dve.wait_ge(cw_ready, i + 1)
                    dve.tensor_scalar(tmp_b, tmp_a, cw[:, 2, hh:hh + 1], None, ALU.mult).then_inc(conv_tap, 1)
                    for n, back in ((0, 2), (1, 1)):
                        dve.wait_ge(conv_tap, 3 * head + n + 1)
                        dve.scalar_tensor_tensor(tmp_b[:, back:], tmp_a[:, :SEQ - back], cw[:, n, hh:hh + 1],
                                                 tmp_b[:, back:], ALU.mult, ALU.add).then_inc(conv_tap, 1)
                    after(st("x", 1))
                    for j in range(TT):
                        dve.wait_ge(score_done, 4 * head + j + 1)
                        diagonal = ps[j][:, j * P:(j + 1) * P]
                        dve.tensor_tensor(diagonal, diagonal, mask, ALU.add).then_inc(masked, 1)
                    for j in range(TT):
                        dve.wait_ge(masked, 4 * head + j + 1)
                        dve.reduce_max(mx[:, j:j + 1], ps[j][:, 0:(j + 1) * P], AX_X).then_inc(max_taken, 1)
                    dve.wait_ge(max_taken, 4 * head + 4)
                    dve.tensor_scalar(nmx[:], mx[:], -SCALE, None, ALU.mult).then_inc(max_ready, 1)
                    dve.wait_ge(exp_done, 4 * head + 4)
                    dve.reciprocal(rsum[:], psum_p[:]).then_inc(sum_inv, 1)
                    dve.wait_ge(sum_inv, head + 1)
                    for j in range(TT):
                        p_j = prob[:, P_OFF[j]:P_OFF[j + 1]]
                        dve.tensor_scalar(p_j, p_j, rsum[:, j:j + 1], None, ALU.mult).then_inc(p_ready, 1)
                    after(st("b"))
                    wait_stage(dve, stage_used, st("b", 1))
                    dve.wait_ge(conv_tap, 3 * head + 3)
                    dve.tensor_tensor(tmp_a, ps[B_B][:], tmp_b, ALU.mult).then_inc(b_used, 1)
                    after(st("b", 1))
                    low_of(ml[:, 2 * hh + 1, :], tmp_a, mh[:, 2 * hh + 1, :], conv_hi, head + 1, conv_lo)
                    for n in range(3):
                        a, b = PT_OFF[n], PT_OFF[n + 1 if n < 2 else 4]
                        low_of(ptl[:, a:b], ps[B_PT[n]][:, 0:b - a], pth[:, a:b], pt_hi, 3 * head + n + 1, pt_lo)

            heads((S_ITER0, 0), 0, IT0, True)
            with dve.Fori(1, HEADS // 2) as i:
                heads((S_HEADS, i), i, ITN, False)
            low_of(ml[:, 2, :], ps[B_PV][:], mh[:, 2, :], pv_hi, HEADS, pv_lo)
            add_out((S_OUT_LAST, 0), HEADS // 2 - 1, 0)

            statistics(0)

            def full(k):
                dve.wait_ge(n_turned, k + 1)
                if k >= 2:
                    dve.wait_ge(n_lo, k - 1)
                dve.tensor_scalar(scr[:, 4 + k % 2, :], ps[4 + k % 4][:], vec[:, G1 + k:G1 + k + 1],
                                  vec[:, B1 + k:B1 + k + 1], ALU.mult, ALU.add).then_inc(n_full, 1)

            for n in range(NB):
                for t in range(TT):
                    block_ = res[:, t, n * 512:(n + 1) * 512]
                    dve.tensor_scalar(block_, block_, mv[:, t, 0:1], rstd[:, t:t + 1],
                                      ALU.subtract, ALU.mult).then_inc(normed, 1)
                for k in range(4 * n, 4 * n + 4):
                    full(k)
                    if k > 0:
                        low_of(xl[:, k - 1, :], scr[:, 4 + (k - 1) % 2, :], xh[:, k - 1, :], n_hi, k, n_lo)
            low_of(xl[:, KT - 1, :], scr[:, 4 + (KT - 1) % 2, :], xh[:, KT - 1, :], n_hi, KT, n_lo)

            def taps(y, bank, side, q, scaled, tap, conv, n):
                dve.wait_ge(scaled, n + 1)
                for k, back, s in ((0, 2, tap), (1, 1, conv)):
                    if k == 1:
                        dve.wait_ge(tap, n + 1)
                    dve.scalar_tensor_tensor(y[:, back:], ps[bank][:, :SEQ - back], fw[:, k, side, q:q + 1],
                                             y[:, back:], ALU.mult, ALU.add).then_inc(s, 1)

            def gates(stage, q, c):
                after(stage)
                taps(yg, 4 + 2 * (q % 2), 0, q, g_scaled, g_tap, g_conv, 4 * c + q)
                after(ahead(stage, 1))
                after(ahead(stage, 2))
                taps(yu, 5 + 2 * (q % 2), 1, q, u_scaled, u_tap, u_conv, 4 * c + q)
                dve.wait_ge(u_conv, 4 * c + q + 1)
                dve.wait_ge(silu_done, 4 * c + q + 1)
                dve.tensor_tensor(a_f, sg, yu, ALU.mult).then_inc(act_full, 1)
                after(ahead(stage, 3))

            def act_low(q, c):
                low_of(ml[:, q, :], a_f, mh[:, q, :], act_hi, 4 * c + q + 1, act_lo)

            def chunk_taps(c):
                dve.tensor_copy(fw[:], fcw[:].rearrange("p k (g f) -> p k g f", g=2)[
                    :, :, :, bass.ds(4 * c, 4)]).then_inc(fw_ready, 1)
                dve.wait_ge(fw_ready, c + 1)

            chunk_taps(0)
            for q in range(4):
                gates((S_CHUNK0 + 4 * q, 0), q, 0)
                act_low(q, 0)
            with dve.Fori(1, CHUNKS) as c:
                chunk_taps(c)
                gates((S_CHUNKS, c), 0, c)
                dve.wait_ge(res_ready, TT)
                add_out((S_CHUNKS + 4, c), c - 1 + HEADS // 2, None)
                act_low(0, c)
                for q in range(1, 4):
                    gates((S_CHUNKS + 8 + 4 * q, c), q, c)
                    act_low(q, c)
            add_out((S_DOWN_LAST, 0), CHUNKS - 1 + HEADS // 2, 1)

            dve.wait_ge(gb_landed, 64)
            statistics(1)
            for t in range(TT):
                dve.tensor_scalar(res[:, t, :], res[:, t, :], mv[:, t, 0:1], rstd[:, t:t + 1],
                                  ALU.subtract, ALU.mult).then_inc(ln2_step, 1)
                dve.wait_ge(ln2_step, 2 * t + 1)
                dve.tensor_tensor(res[:, t, :], res[:, t, :], gb[:, 2, :], ALU.mult).then_inc(ln2_step, 1)
                dve.wait_ge(ln2_step, 2 * t + 2)
                dve.tensor_tensor(res[:, t, :], res[:, t, :], gb[:, 3, :], ALU.add).then_inc(out_ready, 1)

        @block.gpsimd
        def _(pool):
            pool.wait_ge(xl_ready, KT)
            for t in range(TT):
                pool.tensor_scalar(res[:, t, :], res[:, t, :], ALPHA, None, ALU.mult).then_inc(x_scaled, 1)
            pool.wait_ge(gb_landed, 64)
            pool.wait_ge(n_turned, KT)
            for t in range(TT):
                pool.tensor_tensor(res[:, t, :], res[:, t, :], gb[:, 0, :], ALU.mult).then_inc(res_step, 1)
                pool.wait_ge(res_step, 2 * t + 1)
                pool.tensor_tensor(res[:, t, :], res[:, t, :], gb[:, 1, :], ALU.add).then_inc(res_step, 1)
                pool.wait_ge(res_step, 2 * t + 2)
                pool.tensor_scalar(res[:, t, :], res[:, t, :], ALPHA, None, ALU.mult).then_inc(res_ready, 1)


INPUTS = ["x", "positions", "w_in", "q_norm_g", "w_uq", "kv_norm_g", "w_ukv", "conv_w", "w_out", "ln1_g",
          "ln1_b", "w_gate_up", "ffn_conv_w", "w_down", "ln2_g", "ln2_b"]


def kernel(**inputs):
    import concourse.bacc as bacc
    from concourse.bass_utils import run_bass_kernel_spmd

    nc = bacc.Bacc("TRN2", target_bir_lowering=False, num_devices=1, dynamic_dma_scratch_size=1024)
    arrays = {"in_consts": shape_constants()}
    for name in INPUTS:
        arrays[f"in_{name}"] = np.ascontiguousarray(inputs[name])
    args = [nc.dram_tensor(name, a.shape, mybir.dt.from_np(a.dtype), kind="ExternalInput").ap()
            for name, a in arrays.items()]
    out = nc.dram_tensor("out", (1, SEQ, D_MODEL), F32, kind="ExternalOutput").ap()
    hybrid_layer(nc, *args, out)
    r = run_bass_kernel_spmd(nc, [arrays], core_ids=[0])
    return r.results[0]["out"]
```

```python
import math
from contextlib import ExitStack

import numpy as np

import concourse.bass as bass
from concourse import mybir

ALU = mybir.AluOpType
ACT = mybir.ActivationFunctionType
AX_X = mybir.AxisListType.X
F32 = mybir.dt.float32
F32R = mybir.dt.float32r
I32 = mybir.dt.int32

P = 128
D_MODEL = 2048
SEQ = 512
HEADS = 8
NOPE = 128
ROPE = 64
HALF = ROPE // 2
VDIM = 128
Q_RANK = 512
KV_RANK = 256
CONV_WIDTH = D_MODEL - HEADS * VDIM
FFN = 5632
K = 3
LN_EPS = 1e-5
RMS_EPS = 1e-6
ALPHA = 2.0 ** 0.25
SCALE = float(NOPE + ROPE) ** -0.5
ROPE_THETA = 10000.0

KT = D_MODEL // P
TT = SEQ // P
NB = D_MODEL // 512
QT = Q_RANK // P
KVT = KV_RANK // P
FT = FFN // P
KV_COL = Q_RANK
KR_COL = Q_RANK + KV_RANK
B_COL = KR_COL + ROPE
C_COL = B_COL + CONV_WIDTH
X_COL = C_COL + CONV_WIDTH

PERIOD = 24
RAW = 4
SPLIT = 3
STAGE = 1024
S_ITER0 = 2 * (QT + KVT + 1)
S_HEADS = S_ITER0 + 16 - PERIOD
S_OUT_LAST = S_HEADS + PERIOD * (HEADS // 2)
S_CHUNK0 = S_OUT_LAST + 8
S_CHUNKS = S_CHUNK0 + 16 - PERIOD
S_SPARE = S_CHUNK0 + 3
CHUNKS = FT // 4
S_LAST_CHUNK = S_CHUNKS + PERIOD * (CHUNKS - 1)
S_DOWN_LAST = S_LAST_CHUNK + PERIOD
S_END = S_DOWN_LAST + 8
N_ANGLE = 17
assert PERIOD % RAW == 0 and PERIOD % SPLIT == 0

IT0 = [dict(c=0, ukv=2, uq=3, x=4, b=6), dict(c=8, ukv=10, uq=11, x=12, b=14)]
ITN = [dict(c=0, ukv=2, uq=3, out=4, x=12, b=14), dict(c=16, ukv=18, uq=19, x=20, b=22)]

G1, B1, CW, QG, KVG = 0, KT, 2 * KT, 2 * KT + K * 8, 2 * KT + K * 8 + QT
N_ROWS = KVG + KVT


def shape_constants():
    c = np.zeros((P, 2 * P + 1), np.float32)
    c[:, :P] = np.eye(P)
    c[:, P:2 * P] = np.where(np.arange(P)[None, :] <= np.arange(P)[:, None], 0.0, -1e30)
    freq = np.float64(ROPE_THETA) ** (-np.arange(0, ROPE, 2) / ROPE)
    c[:, 2 * P] = np.concatenate([freq, -freq] * 2).astype(np.float32)
    return c


def two_pi_parts():
    parts, rest = [], 2.0 * math.pi
    for _ in range(3):
        unit = 2.0 ** (math.floor(math.log2(rest)) - 10)
        parts.append(math.floor(rest / unit) * unit)
        rest -= parts[-1]
    return parts + [rest]


SHORT = {S_ITER0 - 2: 8 * ROPE, S_ITER0 - 1: 8 * ROPE,
         S_ITER0 + IT0[1]["ukv"]: KVT * NOPE, S_ITER0 + IT0[1]["uq"]: QT * NOPE}
SHORT_LOOPED = {S_HEADS + ITN[1]["ukv"]: KVT * NOPE, S_HEADS + ITN[1]["uq"]: QT * NOPE}


def hybrid_layer(nc, consts, x, positions, w_in, q_norm_g, w_uq, kv_norm_g, w_ukv, conv_w, w_out,
                 ln1_g, ln1_b, w_gate_up, ffn_conv_w, w_down, ln2_g, ln2_b, out):
    with ExitStack() as ctx:
        def sb(name, shape, dt=F32, stack=ctx):
            return stack.enter_context(nc.sbuf_tensor(name, shape, dt))

        def sem(name):
            return ctx.enter_context(nc.semaphore(name))

        const = sb("const", [P, 2 * P + 1])
        ident, mask, freq = const[:, 0:P], const[:, P:2 * P], const[:, 2 * P:2 * P + 1]
        ones = sb("ones", [P, P])
        eps = sb("eps", [P, 2])
        vec = sb("vec", [P, N_ROWS])
        fcw = sb("fcw", [P, K, 2 * FT])
        fw = sb("fw", [P, K, 2, 4])
        cw = sb("cw", [P, K, 2])
        stat = sb("stat", [P, TT, NB, 6])
        mv = sb("mv", [P, TT, 2])
        std = sb("std", [P, TT])
        rstd = sb("rstd", [P, TT])
        shift = sb("shift", [P, TT])
        spare = sb("spare", [P, 1])
        mx = sb("mx", [P, TT])
        nmx = sb("nmx", [P, TT])
        psum_p = sb("psum_p", [P, TT])
        rsum = sb("rsum", [P, TT])
        res = sb("res", [P, TT, D_MODEL])
        xh = sb("xh", [P, KT, SEQ], F32R)
        xl = sb("xl", [P, KT, SEQ], F32R)
        mh = sb("mh", [P, 4, SEQ], F32R)
        ml = sb("ml", [P, 4, SEQ], F32R)
        scr = sb("scr", [P, 6, SEQ])
        raw = sb("raw", [P, RAW, STAGE])
        wh = sb("wh", [P, SPLIT, STAGE], F32R)
        wl = sb("wl", [P, SPLIT, STAGE], F32R)
        with ExitStack() as heads_only:
            cqh = sb("cqh", [P, QT, SEQ], F32R, heads_only)
            cql = sb("cql", [P, QT, SEQ], F32R, heads_only)
            ckh = sb("ckh", [P, KVT, SEQ], F32R, heads_only)
            ckl = sb("ckl", [P, KVT, SEQ], F32R, heads_only)
            krh = sb("krh", [P, SEQ], F32R, heads_only)
            krl = sb("krl", [P, SEQ], F32R, heads_only)
            cosines = sb("cosines", [P, SEQ], F32, heads_only)
            sines = sb("sines", [P, SEQ], F32, heads_only)
            att = sb("att", [P, 5 * SEQ], F32R, heads_only)
            qp1 = sb("qp1", [P, SEQ], F32R, heads_only)
            with ExitStack() as latents_only:
                sqs = sb("sqs", [P, 4, SEQ], F32, latents_only)
            vals = sb("vals", [P, 4, SEQ], F32R, heads_only)
        with ExitStack() as ffn_only:
            gb = sb("gb", [P, 4, D_MODEL], F32, ffn_only)
            mh2 = sb("mh2", [P, 4, SEQ], F32R, ffn_only)
            ml2 = sb("ml2", [P, 4, SEQ], F32R, ffn_only)
        wdh, wdl = (v[:].rearrange("p (s a) n -> p s (a n)", a=2) for v in (xh, xl))
        vh, vl = (vals[:, 2 * j:2 * j + 2, :].rearrange("p h (t n) -> p (h t) n", n=2 * VDIM) for j in range(2))
        qnh, qnl, knh, knl, qp0 = (att[:, j * SEQ:(j + 1) * SEQ] for j in range(5))
        qp = [qp0, qp1[:]]
        PT_OFF = [0, 512, 896, 1152, 1280]
        pth, ptl = att[:, 0:1280], att[:, 1280:2560]
        P_OFF = [0, 128, 384, 768, 1280]
        scr_flat = scr[:].rearrange("p a b -> p (a b)")
        prob = scr_flat[:, 0:1280]
        c_sb = scr_flat[:, 1280:1792]
        tmp_a = scr_flat[:, 1792:2304]
        tmp_b = scr_flat[:, 2304:2816]
        lat = [scr[:, j, :] for j in range(6)]
        rows = scr[:, 0, 0:P]
        frows = scr[:, 0, P:P + K * P].rearrange("p (k n) -> p k n", k=K)
        pos = scr[:, 1, :]
        ang, turns, turns_hi, turns_lo = (scr[:, j, :] for j in (2, 3, 4, 5))
        yg, yu, sg, a_f = (scr[:, j, :] for j in range(4))

        ps = [ctx.enter_context(nc.psum_tensor(f"bank{b}", [P, 512], F32)) for b in range(8)]
        B_LAT = [2, 3, 0, 1, 2, 3]
        B_KR, B_RMS = 4, [5, 6]
        B_C, B_PV, B_KN, B_QN, B_QR, B_X, B_B = 0, 1, 4, 6, 7, 4, 5
        B_V = [5, 2]
        B_PT = [6, 7, 4]
        B_LAST_PV = 5

        raw_landed = [sem(f"raw_landed{j}") for j in range(RAW)]
        x_landed = [sem(f"x_landed{t}") for t in range(TT)]
        (const_landed, rows_landed, pos_landed, rope_landed, gb_landed, out_written) = map(
            sem, ("const_landed", "rows_landed", "pos_landed", "rope_landed", "gb_landed", "out_written"))
        (stage_used, rows_turned, x_turned, rms_sum, score_done, pt_done, pv_done, out_done, n_turned,
         last_done) = map(
            sem, ("stage_used", "rows_turned", "x_turned", "rms_sum", "score_done", "pt_done", "pv_done",
                  "out_done", "n_turned", "last_done"))
        (split_hi, xh_ready, lat_squared, rms_root, lat_hi, cs_ready, kr_hi, c_copied, kn_hi, v_hi, qn_hi,
         qr_hi, exp_done, conv_hi, pt_hi, pv_hi, std_ready, normed_act, n_hi, g_scaled, u_scaled, silu_done,
         act_hi, out_normed) = map(
            sem, ("split_hi", "xh_ready", "lat_squared", "rms_root", "lat_hi", "cs_ready", "kr_hi",
                  "c_copied", "kn_hi", "v_hi", "qn_hi", "qr_hi", "exp_done", "conv_hi", "pt_hi", "pv_hi",
                  "std_ready", "normed_act", "n_hi", "g_scaled", "u_scaled", "silu_done", "act_hi", "out_normed"))
        (split_lo, set_up, angle_step, vec_ready, xl_ready, sq_added, rms_inv, lat_normed, lat_lo,
         kr_prod, kr_rot, kr_lo) = map(
            sem, ("split_lo", "set_up", "angle_step", "vec_ready", "xl_ready", "sq_added", "rms_inv",
                  "lat_normed", "lat_lo", "kr_prod", "kr_rot", "kr_lo"))
        (cw_ready, kn_lo, v_lo, qn_lo, qr_prod, qr_rot, qr_lo, x_used, conv_tap, b_used, conv_lo, masked,
         max_taken, max_ready, sum_inv, p_ready, pt_lo, pv_lo, out_added) = map(
            sem, ("cw_ready", "kn_lo", "v_lo", "qn_lo", "qr_prod", "qr_rot", "qr_lo", "x_used", "conv_tap",
                  "b_used", "conv_lo", "masked", "max_taken", "max_ready", "sum_inv", "p_ready", "pt_lo",
                  "pv_lo", "out_added"))
        (stats_taken, var_ready, rstd_ready, shift_ready, normed_dve, n_full, n_lo, fw_ready, g_tap, g_conv,
         u_tap, u_conv, act_full, act_lo, out_gained, out_ready_dve) = map(
            sem, ("stats_taken", "var_ready", "rstd_ready", "shift_ready", "normed_dve", "n_full", "n_lo",
                  "fw_ready", "g_tap", "g_conv", "u_tap", "u_conv", "act_full", "act_lo", "out_gained",
                  "out_ready_dve"))
        (x_scaled, n_lo_pool, res_step, res_ready, out_ready) = map(
            sem, ("x_scaled", "n_lo_pool", "res_step", "res_ready", "out_ready"))

        def ahead(stage, n):
            return (stage[0] + n, stage[1])

        def wait_stage(eng, s, stage, back=0):
            number, i = stage
            if number + 1 - back > 0:
                eng.wait_ge(s, number + 1 - back + PERIOD * i)

        def split_slot(stage):
            number, i = stage
            if isinstance(i, int) and number == S_SPARE:
                return [v[:, 0:2, :].rearrange("p k n -> p (k n)") for v in (mh, ml)]
            if isinstance(i, int) and number >= S_DOWN_LAST:
                return [v[:, number - S_DOWN_LAST, :] for v in (wdh, wdl)]
            return [v[:, number % SPLIT, :] for v in (wh, wl)]

        def length(stage):
            number, i = stage
            return (SHORT if isinstance(i, int) else SHORT_LOOPED).get(number, STAGE)

        def split_high(stage):
            number, i = stage
            if isinstance(i, int) and number >= S_END:
                return
            act = nc.scalar
            act.wait_ge(raw_landed[number % RAW], 16 * (number // RAW + 1) + 16 * (PERIOD // RAW) * i)
            if isinstance(i, int) and number >= S_DOWN_LAST:
                wait_stage(act, stage_used, (S_DOWN_LAST - 9, 0))
            elif isinstance(i, int) and number == S_SPARE:
                wait_stage(act, stage_used, (S_CHUNK0 - 1, 0))
            else:
                wait_stage(act, stage_used, stage, back=SPLIT)
            if number == (S_ITER0 + IT0[0]["uq"] if isinstance(i, int) else S_HEADS + ITN[0]["uq"]):
                act.wait_ge(rope_landed, 16 + 16 * i)
            n = length(stage)
            act.copy(split_slot(stage)[0][:, 0:n], raw[:, number % RAW, 0:n]).then_inc(split_hi, 1)

        def split_low(stage):
            number, i = stage
            if isinstance(i, int) and number >= S_END:
                return
            dve = nc.vector
            wait_stage(dve, split_hi, stage)
            n = length(stage)
            h, low = split_slot(stage)
            dve.tensor_tensor(low[:, 0:n], raw[:, number % RAW, 0:n], h[:, 0:n].bitcast(F32),
                              ALU.subtract).then_inc(split_lo, 1)

        def pair_banks(q, crossed=False):
            return (0, 1) if crossed else (4 + 2 * (q % 2), 5 + 2 * (q % 2))

        def beside_last(n):
            first = S_LAST_CHUNK + 16
            if n < 5:
                return [(first + n + SPLIT, 0)]
            return [(S_DOWN_LAST + k, 0) for k in ((0, 1, 2), (3, 4, 5), (6, 7))[n - 5]]

        def on_dve(t, n):
            return t == TT - 1 and n >= 2

        block = ctx.enter_context(nc.Block())

        @block.sync
        def _(sp):
            w_in_t = w_in[0].rearrange("(h k p) n -> h p k n", h=2, p=P)
            w_uq_t = w_uq[0].rearrange("(k p) n -> p k n", p=P)
            w_ukv_t = w_ukv[0].rearrange("(k p) n -> p k n", p=P)
            w_out_t = w_out[0].rearrange("(g h p) n -> p g h n", g=2, p=P)
            w_gu_t = w_gate_up[0].rearrange("(h k p) n -> h p k n", h=2, p=P)
            w_down_t = w_down[0].rearrange("(k p) n -> p k n", p=P)

            def load(stage, rows_, start, count, source, row=None):
                number, i = stage
                row = row or count
                dst = raw[:, number % RAW, 0:rows_ * row].rearrange("p (k n) -> p k n", n=row)[:, :, 0:count]
                at = start if isinstance(start, int) else sp.snap(start)
                wait_stage(sp, split_lo, stage, back=RAW)
                sp.dma_start(dst, source(at)).then_inc(raw_landed[number % RAW], 16)

            def load_in(stage, column, width=P, halves=(0, 1)):
                for h in halves:
                    load(ahead(stage, h), 8, column, width, lambda at: w_in_t[h][:, :, bass.ds(at, width)])

            def load_out(stage, i):
                for n in range(NB):
                    for j in range(2):
                        load(ahead(stage, 2 * n + j), 2, 2 * i + j, 512, lambda at: w_out_t[
                            :, :, bass.ds(at, 1), n * 512:(n + 1) * 512].rearrange("p g h n -> p (g h) n"))

            def load_down(stage, c):
                for n in range(NB):
                    for j in range(2):
                        load(ahead(stage, 2 * n + j), 2, 4 * c + 2 * j, 512, lambda at: w_down_t[
                            :, bass.ds(at, 2), n * 512:(n + 1) * 512])

            def load_heads(base, i, table):
                for hh, at in enumerate(table):
                    head = 2 * i + hh
                    load_in(ahead(base, at["c"]), C_COL + P * head)
                    both = hh == 0
                    kv, q = (2 * (NOPE + VDIM), NOPE + ROPE) if both else (NOPE, NOPE)
                    load(ahead(base, at["ukv"]), KVT, 512 * i, kv,
                         lambda a: w_ukv_t[:, :, 256 * hh:][:, :, bass.ds(a, kv)])
                    load(ahead(base, at["uq"]), QT, 384 * i, q, lambda a: w_uq_t[:, :, 192 * hh:][:, :, bass.ds(a, q)],
                         NOPE + 2 * ROPE if both else NOPE)
                    if both:
                        slot = raw[:, (base[0] + at["uq"]) % RAW, :].rearrange("p (k n) -> p k n", k=QT)
                        sp.dma_start(slot[:, :, NOPE + ROPE:], w_uq_t[:, :, 192 + NOPE:][
                            :, :, bass.ds(384 * i, ROPE)]).then_inc(rope_landed, 16)
                    if "out" in at:
                        load_out(ahead(base, at["out"]), i - 1)
                    load_in(ahead(base, at["x"]), X_COL + P * head)
                    load_in(ahead(base, at["b"]), B_COL + P * head)

            def load_pair(stage, tile):
                for j in range(2):
                    for h in range(2):
                        load(ahead(stage, 2 * j + h), 8, j * FFN + P * tile, P,
                             lambda at: w_gu_t[h][:, :, bass.ds(at, P)])

            def load_crossed(stage, tile):
                for h in range(2):
                    for j in range(2):
                        load(ahead(stage, 2 * h + j), 8, j * FFN + P * tile, P,
                             lambda at: w_gu_t[h][:, :, bass.ds(at, P)])

            for t in range(TT):
                if t == TT - 1:
                    load_in((0, 0), KV_COL, halves=(0,))
                sp.dma_start(res[:, t, :], x[0, t * P:(t + 1) * P, :]).then_inc(x_landed[t], 16)
            load_in((0, 0), KV_COL, halves=(1,))
            load_in((2, 0), KV_COL + P)
            for j in range(QT):
                load_in((4 + 2 * j, 0), j * P)
            load_in((12, 0), KR_COL, ROPE)
            load_heads((S_ITER0, 0), 0, IT0)
            with sp.Fori(1, HEADS // 2) as i:
                load_heads((S_HEADS, i), i, ITN)
            load_out((S_OUT_LAST, 0), HEADS // 2 - 1)
            load_crossed((S_CHUNK0, 0), 0)
            for q in range(1, 3):
                load_pair((S_CHUNK0 + 4 * q, 0), q)
            sp.wait_ge(pv_done, HEADS)
            for j, v in enumerate((ln1_g, ln1_b, ln2_g, ln2_b)):
                sp.dma_start(gb[:, j, :], v[0].partition_broadcast(P)).then_inc(gb_landed, 16)
            load_pair((S_CHUNK0 + 12, 0), 3)
            with sp.Fori(1, CHUNKS - 1) as c:
                load_pair((S_CHUNKS, c), 4 * c)
                load_down((S_CHUNKS + 4, c), c - 1)
                for q in range(1, 4):
                    load_pair((S_CHUNKS + 8 + 4 * q, c), 4 * c + q)
            for q in range(4):
                load_pair((S_LAST_CHUNK + 4 * q, 0), 4 * (CHUNKS - 1) + q)
            load_down((S_LAST_CHUNK + 16, 0), CHUNKS - 2)
            load_down((S_DOWN_LAST, 0), CHUNKS - 1)
            for t in range(TT):
                for n in range(NB):
                    if on_dve(t, n):
                        sp.wait_ge(out_ready_dve, n - 1)
                    else:
                        sp.wait_ge(out_ready, 4 * t + n + 1)
                    cols = slice(n * 512, (n + 1) * 512)
                    sp.dma_start(out[0, t * P:(t + 1) * P, cols], res[:, t, cols]).then_inc(out_written, 16)
            sp.wait_ge(out_written, 16 * TT * NB)

        @block.tensor
        def _(pe):
            def pieces3(stage, width):
                return [v.rearrange("p (k n) -> p k n", n=width)
                        for v in split_slot(stage)]

            def products(dst, pairs):
                for n, (sh, sl, vh_, vl_) in enumerate(pairs):
                    pe.matmul(dst, sh, vh_, start=(n == 0), stop=False)
                    pe.matmul(dst, sl, vh_, start=False, stop=False)
                    last = pe.matmul(dst, sh, vl_, start=False, stop=(n == len(pairs) - 1))
                return last

            def project(stage, bank, first=False):
                for h in range(2):
                    st = ahead(stage, h)
                    wait_stage(pe, split_lo, st)
                    w3h, w3l = pieces3(st, P)
                    for k in range(8):
                        kk = 8 * h + k
                        if first and kk % 4 == 0:
                            pe.wait_ge(xl_ready, 4 * (TT - 1) + kk // 4 + 1)
                        for j, (w, v) in enumerate(((w3h, xh), (w3l, xh), (w3h, xl))):
                            last = pe.matmul(ps[bank][:], w[:, k, :], v[:, kk, :],
                                             start=(kk == 0 and j == 0), stop=(kk == KT - 1 and j == 2))
                    last.then_inc(stage_used, 1)

            def project_out(stage, m, first):
                for n in range(NB):
                    for j in range(2):
                        st = ahead(stage, 2 * n + j)
                        wait_stage(pe, split_lo, st)
                        w3h, w3l = pieces3(st, 512)
                        if n == 0:
                            first(j)
                        for t in range(TT):
                            if j == 0 and n > 0:
                                pe.wait_ge(out_added, 16 * m + 4 * (n - 1) + t + 1)
                            tok = slice(t * P, (t + 1) * P)
                            for k in range(2):
                                slot = 2 * j + k
                                for q, (v, w) in enumerate(((mh, w3h), (ml, w3h), (mh, w3l))):
                                    last = pe.matmul(ps[t][:], v[:, slot, tok], w[:, k, :],
                                                     start=(slot == 0 and q == 0),
                                                     stop=(slot == 3 and q == 2))
                            if j == 1 and t < TT - 1:
                                last.then_inc(out_done, 1)
                        last.then_inc(stage_used, 1)

            pe.wait_ge(const_landed, 16)
            for t in range(TT):
                pe.wait_ge(x_landed[t], 16)
                for g in range(4):
                    if t > 0:
                        pe.wait_ge(xl_ready, 4 * (t - 1) + g + 1)
                    for k in range(4):
                        last = pe.transpose(ps[4 + g][:, k * P:(k + 1) * P],
                                            res[:, t, (4 * g + k) * P:(4 * g + k + 1) * P], ident)
                    last.then_inc(x_turned, 1)
            for j in range(6):
                if j == 2:
                    pe.wait_ge(vec_ready, 2)
                if j >= 4:
                    pe.wait_ge(lat_squared, j - 3)
                project((2 * j, 0), B_LAT[j], j == 0)
                if j == 0:
                    pe.wait_ge(rows_landed, 16 * 6)
                    pe.transpose(ps[0][:, 0:N_ROWS], rows[0:N_ROWS, :], ident[0:N_ROWS, 0:N_ROWS]).then_inc(rows_turned, 1)
                    for k in range(K):
                        last = pe.transpose(ps[1][:, k * 2 * FT:(k + 1) * 2 * FT], frows[0:2 * FT, k, :],
                                            ident[0:2 * FT, 0:2 * FT])
                    last.then_inc(rows_turned, 1)
                if j == 2:
                    pe.wait_ge(sq_added, 1)
                    pe.matmul(ps[B_RMS[0]][:], ones[:], sqs[:, 2, :], start=True, stop=True).then_inc(rms_sum, 1)
            for h in range(2):
                wait_stage(pe, split_lo, (12 + h, 0))
                w3h, w3l = pieces3((12 + h, 0), ROPE)
                for k in range(8):
                    kk = 8 * h + k
                    for j, (w, v) in enumerate(((w3h, xh), (w3l, xh), (w3h, xl))):
                        last = pe.matmul(ps[B_KR][0:ROPE, :], w[:, k, :], v[:, kk, :],
                                         start=(kk == 0 and j == 0), stop=(kk == KT - 1 and j == 2))
                last.then_inc(stage_used, 1)
                if h == 0:
                    pe.wait_ge(sq_added, 4)
                    pe.matmul(ps[B_RMS[1]][:], ones[:], sqs[:, 3, :], start=True, stop=True).then_inc(rms_sum, 1)

            def values(head, hh, bank=B_PV):
                n = 0
                for j in range(TT):
                    pe.wait_ge(pt_lo, 3 * head + min(j, 2) + 1)
                    cols = slice(PT_OFF[j], PT_OFF[j + 1])
                    for v, p in ((vh, pth), (vl, pth), (vh, ptl)):
                        last = pe.matmul(ps[bank][:, j * P:512], v[:, j, hh * VDIM:(hh + 1) * VDIM], p[:, cols],
                                         start=(n == 0), stop=(n == 11))
                        n += 1
                last.then_inc(pv_done, 1)

            def heads(base, i, table, first):
                for hh, at in enumerate(table):
                    head = 2 * i + hh
                    project(ahead(base, at["c"]), B_C)
                    if not (first and hh == 0):
                        values(head - 1, 1 - hh)
                    st = ahead(base, at["ukv"])
                    wait_stage(pe, split_lo, st)
                    if first and hh == 0:
                        pe.wait_ge(lat_lo, KVT)
                        pe.wait_ge(kr_prod, 3)
                    else:
                        pe.wait_ge(b_used, head)
                    w3h, w3l = pieces3(st, 2 * (NOPE + VDIM) if hh == 0 else NOPE)
                    last = products(ps[B_KN][:], [(w3h[:, k, 0:NOPE], w3l[:, k, 0:NOPE], ckh[:, k, :], ckl[:, k, :])
                                                  for k in range(KVT)])
                    if hh == 0:
                        pe.wait_ge(lat_squared, 6)
                        if not first:
                            pe.wait_ge(exp_done, 4 * head)
                        w4h, w4l = (w.rearrange("p k (h n) -> p k h n", h=2)[:, :, :, NOPE:] for w in (w3h, w3l))
                        for t in range(TT):
                            tok = slice(t * P, (t + 1) * P)
                            dst = ps[B_V[t // 2]][:, (t % 2) * 256:(t % 2 + 1) * 256].rearrange("p (h n) -> p h n", h=2)
                            last = products(dst, [(ckh[:, k, tok], ckl[:, k, tok], w4h[:, k], w4l[:, k])
                                                  for k in range(KVT)])
                    last.then_inc(stage_used, 1)
                    st = ahead(base, at["uq"])
                    wait_stage(pe, split_lo, st)
                    if first and hh == 0:
                        pe.wait_ge(lat_lo, KVT + QT)
                    w3h, w3l = pieces3(st, NOPE + 2 * ROPE if hh == 0 else NOPE)
                    for bank, a in ((B_QN, 0), (B_QR, NOPE))[0:2 - hh]:
                        last = products(ps[bank][:], [(w3h[:, k, a:a + P], w3l[:, k, a:a + P], cqh[:, k, :], cql[:, k, :])
                                                      for k in range(QT)])
                    last.then_inc(stage_used, 1)
                    if "out" in at:
                        def ready(j):
                            if j == 0:
                                pe.wait_ge(v_lo, 2 * i + 2)
                                pe.wait_ge(c_copied, head + 1)
                                pe.wait_ge(pv_lo, 2 * i)
                                pe.wait_ge(conv_lo, 2 * i)
                        project_out(ahead(base, at["out"]), i - 1, ready)
                    pe.wait_ge(kn_lo, head + 1)
                    project(ahead(base, at["x"]), B_X)
                    pe.wait_ge(v_lo, 2 * i + 2)
                    pe.wait_ge(qn_lo, head + 1)
                    pe.wait_ge(qr_lo, head + 1)
                    if first and hh == 0:
                        pe.wait_ge(kr_lo, 1)
                    if "out" in at:
                        pe.wait_ge(out_added, 16 * i)
                    else:
                        pe.wait_ge(c_copied, head + 1)
                        if not (first and hh == 0):
                            pe.wait_ge(pv_lo, head)
                    for j in range(TT):
                        tok, keys = slice(j * P, (j + 1) * P), slice(0, (j + 1) * P)
                        for n, (a, b) in enumerate(((qnh, knh), (qnl, knh), (qnh, knl), (qp[hh], krh), (qp[hh], krl))):
                            last = pe.matmul(ps[j][:, keys], a[:, tok], b[:, keys], start=(n == 0), stop=(n == 4))
                        last.then_inc(score_done, 1)
                    project(ahead(base, at["b"]), B_B)
                    pe.wait_ge(x_used, head + 1)
                    pe.wait_ge(p_ready, 4 * head + 4)
                    for n, tiles in enumerate(((0,), (1,), (2, 3))):
                        for j in tiles:
                            for q in range(j, TT):
                                to = PT_OFF[j] - PT_OFF[tiles[0]] + (q - j) * P
                                last = pe.transpose(ps[B_PT[n]][:, to:to + P],
                                                    prob[:, P_OFF[q] + j * P:P_OFF[q] + (j + 1) * P], ident)
                        last.then_inc(pt_done, 1)

            heads((S_ITER0, 0), 0, IT0, True)
            with pe.Fori(1, HEADS // 2) as i:
                heads((S_HEADS, i), i, ITN, False)
            def ready(j):
                if j == 0:
                    pe.wait_ge(pv_lo, HEADS - 1)
                    pe.wait_ge(conv_lo, HEADS - 1)
                else:
                    values(HEADS - 1, 1, B_LAST_PV)
                    pe.wait_ge(conv_lo, HEADS)
                    pe.wait_ge(pv_lo, HEADS)
            project_out((S_OUT_LAST, 0), HEADS // 2 - 1, ready)

            def turn(n):
                if n == 0:
                    pe.wait_ge(normed_dve, TT)
                else:
                    pe.wait_ge(normed_act, TT * n)
                for k in range(4 * n, 4 * n + 4):
                    if k >= 4:
                        pe.wait_ge(n_full, k - 3)
                    for t in range(TT):
                        last = pe.transpose(ps[4 + k % 4][:, t * P:(t + 1) * P], res[:, t, k * P:(k + 1) * P], ident)
                    last.then_inc(n_turned, 1)

            def crossed_pair(stage):
                pe.wait_ge(out_added, 16 * (HEADS // 2))
                for h in range(2):
                    for j in range(2):
                        wait_stage(pe, split_lo, ahead(stage, 2 * h + j))
                    parts = [pieces3(ahead(stage, 2 * h + j), P) for j in range(2)]
                    for k in range(8):
                        kk = 8 * h + k
                        if kk % 4 == 0 and kk + 4 < KT:
                            turn(kk // 4 + 1)
                        pe.wait_ge(*((n_lo_pool, (kk + 1) // 2) if kk % 2 else (n_lo, kk // 2 + 1)))
                        for j, (w3h, w3l) in enumerate(parts):
                            for q, (w, v) in enumerate(((w3h, xh), (w3l, xh), (w3h, xl))):
                                last = pe.matmul(ps[j][:], w[:, k, :], v[:, kk, :],
                                                 start=(kk == 0 and q == 0), stop=(kk == KT - 1 and q == 2))
                            if k == 7:
                                last.then_inc(stage_used, 1)

            def pair(stage, q, c, first):
                for j, free in enumerate((g_conv, u_conv)):
                    if first and q < 3:
                        pe.wait_ge(n_full, KT)
                    else:
                        pe.wait_ge(free, 4 * c + q - 1)
                    project(ahead(stage, 2 * j), pair_banks(q)[j])

            def down(stage, c):
                def ready(j):
                    pe.wait_ge(out_added, 16 * (c + HEADS // 2))
                    pe.wait_ge(act_lo, 4 * c + 2 * j + 2)
                project_out(stage, c + HEADS // 2, ready)

            turn(0)
            crossed_pair((S_CHUNK0, 0))
            for q in range(1, 4):
                pair((S_CHUNK0 + 4 * q, 0), q, 0, True)
            with pe.Fori(1, CHUNKS - 1) as c:
                pair((S_CHUNKS, c), 0, c, False)
                down((S_CHUNKS + 4, c), c - 1)
                for q in range(1, 4):
                    pair((S_CHUNKS + 8 + 4 * q, c), q, c, False)
            for q in range(4):
                pair((S_LAST_CHUNK + 4 * q, 0), q, CHUNKS - 1, False)
            down((S_LAST_CHUNK + 16, 0), CHUNKS - 2)
            for t in range(TT):
                tok = slice(t * P, (t + 1) * P)
                for n in range(NB):
                    bank = 4 * ((t + 1) % 2) + n
                    if t == 0:
                        pe.wait_ge(g_conv, FT)
                        pe.wait_ge(u_conv, FT)
                        pe.wait_ge(act_lo, FT)
                    else:
                        m = CHUNKS - 2 + HEADS // 2 if t == 1 else CHUNKS - 1 + HEADS // 2
                        pe.wait_ge(out_added, 16 * m + (12 if t == 1 else 4 * (t - 2)) + n + 1)
                    for k in range(4):
                        if t == 0 and k % 2 == 0:
                            wait_stage(pe, split_lo, (S_DOWN_LAST + 2 * n + k // 2, 0))
                        w3h, w3l = (w[:, 2 * n + k // 2, (k % 2) * 512:(k % 2 + 1) * 512] for w in (wdh, wdl))
                        for q, (v, w) in enumerate(((mh2, w3h), (ml2, w3h), (mh2, w3l))):
                            last = pe.matmul(ps[bank][:], v[:, k, tok], w, start=(k == 0 and q == 0),
                                             stop=(k == 3 and q == 2))
                    last.then_inc(last_done, 1)

        @block.scalar
        def _(act):
            def after(stage):
                split_high(ahead(stage, SPLIT))

            act.dma_start(const[:], consts).then_inc(const_landed, 16)
            for at, v in ((G1, ln1_g[0].rearrange("(k p) -> k p", p=P)), (B1, ln1_b[0].rearrange("(k p) -> k p", p=P)),
                          (CW, conv_w[0].rearrange("k (h p) -> (k h) p", p=P)),
                          (QG, q_norm_g[0].rearrange("(k p) -> k p", p=P)),
                          (KVG, kv_norm_g[0].rearrange("(k p) -> k p", p=P))):
                act.dma_start(rows[at:at + v.shape[0], :], v).then_inc(rows_landed, 16)
            act.dma_start(frows[0:2 * FT], ffn_conv_w[0].rearrange("k (r p) -> r k p", p=P)).then_inc(rows_landed, 16)
            act.dma_start(pos.bitcast(I32), positions[0].partition_broadcast(P)).then_inc(pos_landed, 16)
            for t in range(TT):
                for g in range(4):
                    act.wait_ge(x_turned, 4 * t + g + 1)
                    act.copy(xh[:, 4 * g:4 * g + 4, t * P:(t + 1) * P],
                             ps[4 + g][:].rearrange("p (k n) -> p k n", n=P)).then_inc(xh_ready, 1)
                if t == TT - 2:
                    split_high((0, 0))
            for s in range(1, SPLIT):
                split_high((s, 0))

            def latent(j):
                act.copy(lat[j], ps[B_LAT[j]][:])
                if j >= 2:
                    act.wait_ge(sq_added, 1 if j < 4 else 2)
                act.activation(sqs[:, j % 2, :], ps[B_LAT[j]][:], ACT.Square).then_inc(lat_squared, 1)

            def root(n, rank, dst):
                act.wait_ge(rms_sum, n + 1)
                act.activation(dst, ps[B_RMS[n]][:], ACT.Sqrt, bias=eps[:, 1:2], scale=1.0 / rank).then_inc(rms_root, 1)

            for s in range(2 * (KVT + QT)):
                wait_stage(act, stage_used, (s, 0))
                if s == 1:
                    act.wait_ge(rows_turned, 2)
                if s == 3:
                    act.wait_ge(angle_step, N_ANGLE)
                    act.activation(cosines[:], turns, ACT.Sin)
                    act.activation(sines[:], ang, ACT.Sin).then_inc(cs_ready, 1)
                if s == 5:
                    act.wait_ge(cs_ready, 1)
                if s % 2 == 1:
                    latent(s // 2)
                after((s, 0))
                if s == 5:
                    root(0, KV_RANK, sqs[:, 2, :])
                    for k in range(KVT):
                        act.wait_ge(lat_normed, k + 1)
                        act.copy(ckh[:, k, :], lat[k]).then_inc(lat_hi, 1)
            after((12, 0))
            root(1, Q_RANK, sqs[:, 3, :])
            for k in range(QT):
                act.wait_ge(lat_normed, KVT + k + 1)
                act.copy(cqh[:, k, :], lat[KVT + k]).then_inc(lat_hi, 1)
            after((13, 0))
            act.wait_ge(kr_rot, 1)
            act.copy(krh[0:ROPE, :], sqs[0:ROPE, 0, :])
            act.copy(krh[ROPE:P, :], sqs[0:ROPE, 0, :]).then_inc(kr_hi, 1)

            def values_high(head, slot):
                act.wait_ge(pv_done, head + 1)
                act.copy(mh[:, slot, :], ps[B_PV][:]).then_inc(pv_hi, 1)

            def heads(base, i, table, first):
                for hh, at in enumerate(table):
                    head = 2 * i + hh

                    def st(name, n=0):
                        return ahead(base, at[name] + n)
                    after(st("c"))
                    wait_stage(act, stage_used, st("c", 1))
                    act.copy(c_sb, ps[B_C][:]).then_inc(c_copied, 1)
                    after(st("c", 1))
                    if not (first and hh == 0):
                        values_high(head - 1, 2 * (1 - hh))
                    wait_stage(act, stage_used, st("ukv"))
                    act.copy(knh, ps[B_KN][:]).then_inc(kn_hi, 1)
                    if hh == 0:
                        if first:
                            act.wait_ge(kr_lo, 1)
                        for n in range(2):
                            act.copy(vals[:, n, :], ps[B_V[n]][:]).then_inc(v_hi, 1)
                    after(st("ukv"))
                    wait_stage(act, stage_used, st("uq"))
                    act.copy(qnh, ps[B_QN][:]).then_inc(qn_hi, 1)
                    if hh == 0:
                        for n in range(2):
                            act.wait_ge(qr_rot, head + n + 1)
                            act.copy(qp[n][0:ROPE, :], (tmp_a, tmp_b)[n][0:ROPE, :]).then_inc(qr_hi, 1)
                    after(st("uq"))
                    if "out" in at:
                        for n in range(2 * NB):
                            after(st("out", n))
                    after(st("x"))
                    after(st("x", 1))
                    act.wait_ge(max_ready, head + 1)
                    for j in range(TT):
                        act.activation(prob[:, P_OFF[j]:P_OFF[j + 1]], ps[j][:, 0:(j + 1) * P], ACT.Exp,
                                       bias=nmx[:, j:j + 1], scale=SCALE,
                                       accum_out=psum_p[:, j:j + 1]).then_inc(exp_done, 1)
                    after(st("b"))
                    act.wait_ge(b_used, head + 1)
                    act.copy(mh[:, 2 * hh + 1, :], tmp_a).then_inc(conv_hi, 1)
                    after(st("b", 1))
                    for n in range(3):
                        act.wait_ge(pt_done, 3 * head + n + 1)
                        a, b = PT_OFF[n], PT_OFF[n + 1 if n < 2 else 4]
                        act.copy(pth[:, a:b], ps[B_PT[n]][:, 0:b - a]).then_inc(pt_hi, 1)

            heads((S_ITER0, 0), 0, IT0, True)
            with act.Fori(1, HEADS // 2) as i:
                heads((S_HEADS, i), i, ITN, False)
            after((S_OUT_LAST, 0))
            act.wait_ge(pv_done, HEADS)
            act.copy(mh[:, 2, :], ps[B_LAST_PV][:]).then_inc(pv_hi, 1)
            for n in range(1, 2 * NB):
                after((S_OUT_LAST + n, 0))

            def deviation(n, t):
                act.wait_ge(var_ready, TT * n + t + 1)
                act.activation(std[:, t:t + 1], mv[:, t, 1:2], ACT.Sqrt, bias=eps[:, 0:1]).then_inc(std_ready, 1)

            def normalise(t, n, s):
                block_ = res[:, t, n * 512:(n + 1) * 512]
                act.activation(block_, block_, ACT.Identity, bias=shift[:, t:t + 1],
                               scale=rstd[:, t:t + 1]).then_inc(s, 1)

            act.activation(spare[:], eps[:, 0:1], ACT.Sqrt)
            for t in range(TT):
                deviation(0, t)
            act.wait_ge(shift_ready, TT)
            for n in range(1, NB + 1):
                if n < NB:
                    for t in range(TT):
                        normalise(t, n, normed_act)
                for k in range(4 * n - 4, 4 * n):
                    act.wait_ge(n_full, k + 1)
                    act.copy(xh[:, k, :], scr[:, 2 + k % 4, :]).then_inc(n_hi, 1)
                if n == 1:
                    split_high((S_SPARE, 0))

            def gates(stage, q, c, banks, crossed=False):
                g_end = 2 if crossed else 1
                for n in range(1 if crossed else 0, g_end):
                    after(ahead(stage, n))
                wait_stage(act, stage_used, ahead(stage, g_end))
                act.wait_ge(fw_ready, c + 1)
                act.activation(yg, ps[banks[0]][:], ACT.Copy, scale=fw[:, K - 1, 0, q:q + 1]).then_inc(g_scaled, 1)
                for n in range(g_end, 3):
                    after(ahead(stage, n))
                wait_stage(act, stage_used, ahead(stage, 3))
                act.activation(yu, ps[banks[1]][:], ACT.Copy, scale=fw[:, K - 1, 1, q:q + 1]).then_inc(u_scaled, 1)
                act.wait_ge(g_conv, 4 * c + q + 1)
                act.activation(sg, yg, ACT.Silu).then_inc(silu_done, 1)
                after(ahead(stage, 3))

            def act_high(q, c, dst=mh):
                act.wait_ge(act_full, 4 * c + q + 1)
                act.copy(dst[:, q, :], a_f).then_inc(act_hi, 1)

            for q in range(4):
                gates((S_CHUNK0 + 4 * q, 0), q, 0, pair_banks(q, q == 0), q == 0)
                act_high(q, 0)
            with act.Fori(1, CHUNKS - 1) as c:
                gates((S_CHUNKS, c), 0, c, pair_banks(0))
                for n in range(2 * NB):
                    after((S_CHUNKS + 4 + n, c))
                act_high(0, c)
                for q in range(1, 4):
                    gates((S_CHUNKS + 8 + 4 * q, c), q, c, pair_banks(q))
                    act_high(q, c)
            for q in range(4):
                gates((S_LAST_CHUNK + 4 * q, 0), q, CHUNKS - 1, pair_banks(q))
                act_high(q, CHUNKS - 1, mh2)
            for n in range(2 * NB):
                for stage in beside_last(n):
                    split_high(stage)
            act.activation(spare[:], eps[:, 0:1], ACT.Sqrt)
            for t in range(TT):
                deviation(1, t)
                act.wait_ge(shift_ready, TT + t + 1)
                for n in range(NB):
                    normalise(t, n, out_normed)

        @block.vector
        def _(dve):
            def after(stage):
                split_low(ahead(stage, SPLIT))

            dve.memset(eps[:, 0:1], LN_EPS)
            dve.memset(eps[:, 1:2], RMS_EPS)
            dve.memset(ones[:], 1.0)
            dve.memset(krl[ROPE:P, :].bitcast(F32), 0.0).then_inc(set_up, 1)
            for t in range(TT):
                for g in range(4):
                    dve.wait_ge(xh_ready, 4 * t + g + 1)
                    four = (slice(None), slice(4 * g, 4 * g + 4), slice(t * P, (t + 1) * P))
                    dve.tensor_tensor(xl[four], ps[4 + g][:].rearrange("p (k n) -> p k n", n=P),
                                      xh[four].bitcast(F32), ALU.subtract).then_inc(xl_ready, 1)
                if t == TT - 2:
                    split_low((0, 0))
            for s in range(1, SPLIT):
                split_low((s, 0))

            angle_steps = [0]

            def step(ins):
                angle_steps[0] += 1
                ins.then_inc(angle_step, 1)
                dve.wait_ge(angle_step, angle_steps[0])

            def angles(part):
                if part == 0:
                    dve.wait_ge(pos_landed, 16)
                    step(dve.tensor_copy(ang, pos.bitcast(I32)))
                    step(dve.tensor_scalar(ang, ang, freq, None, ALU.mult))
                    step(dve.tensor_scalar(turns, ang, 1.0 / (2.0 * math.pi), 1.5 * 2.0 ** 23, ALU.mult, ALU.add))
                    step(dve.tensor_scalar(turns, turns, -1.5 * 2.0 ** 23, None, ALU.add))
                    step(dve.tensor_scalar(turns_hi, turns, 1.5 * 2.0 ** 34, None, ALU.add))
                    step(dve.tensor_scalar(turns_hi, turns_hi, -1.5 * 2.0 ** 34, None, ALU.add))
                    step(dve.tensor_tensor(turns_lo, turns, turns_hi, ALU.subtract))
                elif part == 1:
                    parts = two_pi_parts()
                    for size, counts in ((parts[0], (turns_hi, turns_lo)), (parts[1], (turns_hi, turns_lo)),
                                         (parts[2], (turns_hi, turns_lo)), (parts[3], (turns,))):
                        for n in counts:
                            step(dve.scalar_tensor_tensor(ang, n, -size, ang, ALU.mult, ALU.add))
                else:
                    step(dve.tensor_scalar(ang, ang, math.pi, -math.pi, ALU.min, ALU.max))
                    step(dve.scalar_tensor_tensor(turns, ang, -1.0, ang, ALU.mult, ALU.max))
                    step(dve.tensor_scalar(turns, turns, -1.0, math.pi / 2, ALU.mult, ALU.add))
                    assert angle_steps[0] == N_ANGLE, angle_steps

            def norm_latents(n, first, tiles, gain, high, low):
                inv = sqs[:, 2 + n, :]
                dve.wait_ge(rms_root, n + 1)
                dve.reciprocal(inv, inv).then_inc(rms_inv, 1)
                dve.wait_ge(rms_inv, n + 1)
                dve.wait_ge(vec_ready, 1)
                for k in range(tiles):
                    dve.scalar_tensor_tensor(lat[first + k], lat[first + k], vec[:, gain + k:gain + k + 1], inv,
                                             ALU.mult, ALU.mult).then_inc(lat_normed, 1)
                for k in range(tiles):
                    dve.wait_ge(lat_hi, first + k + 1)
                    dve.tensor_tensor(low[:, k, :], lat[first + k], high[:, k, :].bitcast(F32),
                                      ALU.subtract).then_inc(lat_lo, 1)

            for s in range(2 * (KVT + QT)):
                after((s, 0))
                if s < 3:
                    angles(s)
                if s == 1:
                    dve.wait_ge(rows_turned, 1)
                    dve.tensor_copy(vec[:], ps[0][:, 0:N_ROWS]).then_inc(vec_ready, 1)
                    dve.wait_ge(rows_turned, 2)
                    dve.tensor_copy(fcw[:].rearrange("p k n -> p (k n)"), ps[1][:, 0:K * 2 * FT]).then_inc(vec_ready, 1)
                if s % 2 == 1:
                    j = s // 2
                    dve.wait_ge(lat_squared, j + 1)
                    if j == 1:
                        dve.tensor_tensor(sqs[:, 2, :], sqs[:, 0, :], sqs[:, 1, :], ALU.add).then_inc(sq_added, 1)
                    if j == 3:
                        dve.tensor_tensor(sqs[:, 3, :], sqs[:, 0, :], sqs[:, 1, :], ALU.add).then_inc(sq_added, 1)
                    if j > 3:
                        dve.wait_ge(sq_added, j - 2)
                        dve.tensor_tensor(sqs[:, 3, :], sqs[:, 3, :], sqs[:, j % 2, :], ALU.add).then_inc(sq_added, 1)
                if s == 5:
                    norm_latents(0, 0, KVT, KVG, ckh, ckl)
            after((12, 0))
            norm_latents(1, KVT, QT, QG, cqh, cql)
            after((13, 0))

            def rotate(bank, n, dst, crossed, products_):
                dve.tensor_tensor(dst[0:n * ROPE, :], ps[bank][0:n * ROPE, :], cosines[0:n * ROPE, :],
                                  ALU.mult).then_inc(products_, 1)
                for half in range(2 * n):
                    here, there = (slice(h * HALF, (h + 1) * HALF) for h in (half, half ^ 1))
                    dve.tensor_tensor(crossed[there, :], ps[bank][here, :], sines[here, :],
                                      ALU.mult).then_inc(products_, 1)

            dve.wait_ge(cs_ready, 1)
            wait_stage(dve, stage_used, (13, 0))
            rotate(B_KR, 1, sqs[:, 0, :], sqs[:, 1, :], kr_prod)
            dve.wait_ge(kr_prod, 3)
            dve.tensor_tensor(sqs[0:ROPE, 0, :], sqs[0:ROPE, 0, :], sqs[0:ROPE, 1, :], ALU.add).then_inc(kr_rot, 1)
            dve.wait_ge(kr_hi, 1)
            dve.tensor_tensor(krl[0:ROPE, :], sqs[0:ROPE, 0, :], krh[0:ROPE, :].bitcast(F32),
                              ALU.subtract).then_inc(kr_lo, 1)

            def low_of(dst, full, high, have, n, s):
                dve.wait_ge(have, n)
                dve.tensor_tensor(dst, full, high.bitcast(F32), ALU.subtract).then_inc(s, 1)

            def take_statistics(t, n, added):
                dve.wait_ge(out_added, added)
                dve.bn_stats(stat[:, t, n, :], res[:, t, n * 512:(n + 1) * 512]).then_inc(stats_taken, 1)

            def add_out(stage, m, stats=False, then=None):
                then = then or (lambda n: after(ahead(stage, n)))
                for n in range(NB):
                    then(2 * n)
                    for t in range(TT):
                        if t < TT - 1:
                            dve.wait_ge(out_done, 12 * m + 3 * n + t + 1)
                        else:
                            wait_stage(dve, stage_used, ahead(stage, 2 * n + 1))
                        block_ = res[:, t, n * 512:(n + 1) * 512]
                        dve.tensor_tensor(block_, block_, ps[t][:], ALU.add).then_inc(out_added, 1)
                        if stats:
                            take_statistics(t, n, 16 * m + 4 * n + t + 1)
                            if n == NB - 1:
                                variance(t, 4 * n + t + 1)
                    then(2 * n + 1)

            def variance(t, taken):
                dve.wait_ge(stats_taken, taken)
                dve.bn_aggr(mv[:, t, :], stat[:, t, :, :].rearrange("p n s -> p (n s)")).then_inc(var_ready, 1)

            def scaling(norm, t):
                dve.wait_ge(std_ready, TT * norm + t + 1)
                dve.reciprocal(rstd[:, t:t + 1], std[:, t:t + 1]).then_inc(rstd_ready, 1)
                dve.wait_ge(rstd_ready, TT * norm + t + 1)
                dve.scalar_tensor_tensor(shift[:, t:t + 1], mv[:, t, 0:1], -1.0, rstd[:, t:t + 1],
                                         ALU.mult, ALU.mult).then_inc(shift_ready, 1)

            def heads(base, i, table, first):
                dve.tensor_copy(cw[:], vec[:, CW:CW + K * 8].rearrange("p (k h) -> p k h", k=K)[
                    :, :, bass.ds(2 * i, 2)]).then_inc(cw_ready, 1)
                for hh, at in enumerate(table):
                    head = 2 * i + hh

                    def st(name, n=0):
                        return ahead(base, at[name] + n)
                    after(st("c"))
                    after(st("c", 1))
                    if not (first and hh == 0):
                        low_of(ml[:, 2 * (1 - hh), :], ps[B_PV][:], mh[:, 2 * (1 - hh), :], pv_hi, head, pv_lo)
                    low_of(knl, ps[B_KN][:], knh, kn_hi, head + 1, kn_lo)
                    if hh == 0:
                        for n in range(2):
                            low_of(vals[:, 2 + n, :], ps[B_V[n]][:], vals[:, n, :], v_hi, head + n + 1, v_lo)
                    after(st("ukv"))
                    wait_stage(dve, stage_used, st("uq"))
                    if hh == 0:
                        rotate(B_QR, 2, tmp_a, tmp_b, qr_prod)
                        dve.wait_ge(qr_prod, 5 * i + 5)
                        for n, (first_row, dst) in enumerate(((0, tmp_a), (ROPE, tmp_b))):
                            if n == 1:
                                dve.wait_ge(qr_rot, head + 1)
                            rows_ = slice(first_row, first_row + ROPE)
                            dve.tensor_tensor(dst[0:ROPE, :], tmp_a[rows_, :], tmp_b[rows_, :],
                                              ALU.add).then_inc(qr_rot, 1)
                    low_of(qnl, ps[B_QN][:], qnh, qn_hi, head + 1, qn_lo)
                    if hh == 0:
                        for n in range(2):
                            low_of(qp[n][ROPE:P, :], (tmp_a, tmp_b)[n][0:ROPE, :], qp[n][0:ROPE, :],
                                   qr_hi, head + n + 1, qr_lo)
                    after(st("uq"))
                    if "out" in at:
                        dve.wait_ge(x_scaled, TT)
                        add_out(st("out"), i - 1, None)
                    after(st("x"))
                    wait_stage(dve, stage_used, st("x", 1))
                    dve.wait_ge(c_copied, head + 1)
                    dve.wait_ge(qr_lo, 2 * i + 2)
                    dve.tensor_tensor(tmp_a, ps[B_X][:], c_sb, ALU.mult).then_inc(x_used, 1)
                    dve.wait_ge(x_used, head + 1)
                    dve.wait_ge(cw_ready, i + 1)
                    dve.tensor_scalar(tmp_b, tmp_a, cw[:, 2, hh:hh + 1], None, ALU.mult).then_inc(conv_tap, 1)
                    for n, back in ((0, 2), (1, 1)):
                        dve.wait_ge(conv_tap, 3 * head + n + 1)
                        dve.scalar_tensor_tensor(tmp_b[:, back:], tmp_a[:, :SEQ - back], cw[:, n, hh:hh + 1],
                                                 tmp_b[:, back:], ALU.mult, ALU.add).then_inc(conv_tap, 1)
                    after(st("x", 1))
                    for j in range(TT):
                        dve.wait_ge(score_done, 4 * head + j + 1)
                        diagonal = ps[j][:, j * P:(j + 1) * P]
                        dve.tensor_tensor(diagonal, diagonal, mask, ALU.add).then_inc(masked, 1)
                    for j in range(TT):
                        dve.wait_ge(masked, 4 * head + j + 1)
                        dve.reduce_max(mx[:, j:j + 1], ps[j][:, 0:(j + 1) * P], AX_X).then_inc(max_taken, 1)
                    dve.wait_ge(max_taken, 4 * head + 4)
                    dve.tensor_scalar(nmx[:], mx[:], -SCALE, None, ALU.mult).then_inc(max_ready, 1)
                    dve.wait_ge(exp_done, 4 * head + 4)
                    dve.reciprocal(rsum[:], psum_p[:]).then_inc(sum_inv, 1)
                    dve.wait_ge(sum_inv, head + 1)
                    for j in range(TT):
                        p_j = prob[:, P_OFF[j]:P_OFF[j + 1]]
                        dve.tensor_scalar(p_j, p_j, rsum[:, j:j + 1], None, ALU.mult).then_inc(p_ready, 1)
                    after(st("b"))
                    wait_stage(dve, stage_used, st("b", 1))
                    dve.wait_ge(conv_tap, 3 * head + 3)
                    dve.tensor_tensor(tmp_a, ps[B_B][:], tmp_b, ALU.mult).then_inc(b_used, 1)
                    after(st("b", 1))
                    low_of(ml[:, 2 * hh + 1, :], tmp_a, mh[:, 2 * hh + 1, :], conv_hi, head + 1, conv_lo)
                    for n in range(3):
                        a, b = PT_OFF[n], PT_OFF[n + 1 if n < 2 else 4]
                        low_of(ptl[:, a:b], ps[B_PT[n]][:, 0:b - a], pth[:, a:b], pt_hi, 3 * head + n + 1, pt_lo)

            heads((S_ITER0, 0), 0, IT0, True)
            with dve.Fori(1, HEADS // 2) as i:
                heads((S_HEADS, i), i, ITN, False)
            def last_out(n):
                after((S_OUT_LAST + n, 0))
                if n == 0:
                    low_of(ml[:, 2, :], ps[B_LAST_PV][:], mh[:, 2, :], pv_hi, HEADS, pv_lo)

            add_out((S_OUT_LAST, 0), HEADS // 2 - 1, True, last_out)

            for t in range(TT):
                scaling(0, t)
            dve.wait_ge(shift_ready, TT)
            for t in range(TT):
                block_ = res[:, t, 0:512]
                dve.tensor_scalar(block_, block_, rstd[:, t:t + 1], shift[:, t:t + 1],
                                  ALU.mult, ALU.add).then_inc(normed_dve, 1)
            for k in range(KT + 1):
                if k < KT:
                    dve.wait_ge(n_turned, k + 1)
                    if k >= 4:
                        dve.wait_ge(*((n_lo_pool, k // 2 - 1) if k % 2 else (n_lo, k // 2 - 1)))
                    dve.tensor_scalar(scr[:, 2 + k % 4, :], ps[4 + k % 4][:], vec[:, G1 + k:G1 + k + 1],
                                      vec[:, B1 + k:B1 + k + 1], ALU.mult, ALU.add).then_inc(n_full, 1)
                if k % 2 == 1:
                    low_of(xl[:, k - 1, :], scr[:, 2 + (k - 1) % 4, :], xh[:, k - 1, :], n_hi, k, n_lo)
                if k == 3:
                    split_low((S_SPARE, 0))

            def taps(y, bank, side, q, scaled, tap, conv, n):
                dve.wait_ge(scaled, n + 1)
                for k, back, s in ((0, 2, tap), (1, 1, conv)):
                    if k == 1:
                        dve.wait_ge(tap, n + 1)
                    dve.scalar_tensor_tensor(y[:, back:], ps[bank][:, :SEQ - back], fw[:, k, side, q:q + 1],
                                             y[:, back:], ALU.mult, ALU.add).then_inc(s, 1)

            def gates(stage, q, c, banks, crossed=False):
                g_end = 2 if crossed else 1
                for n in range(1 if crossed else 0, g_end):
                    after(ahead(stage, n))
                taps(yg, banks[0], 0, q, g_scaled, g_tap, g_conv, 4 * c + q)
                for n in range(g_end, 3):
                    after(ahead(stage, n))
                taps(yu, banks[1], 1, q, u_scaled, u_tap, u_conv, 4 * c + q)
                dve.wait_ge(u_conv, 4 * c + q + 1)
                dve.wait_ge(silu_done, 4 * c + q + 1)
                dve.tensor_tensor(a_f, sg, yu, ALU.mult).then_inc(act_full, 1)
                after(ahead(stage, 3))

            def act_low(q, c, high=mh, low=ml):
                low_of(low[:, q, :], a_f, high[:, q, :], act_hi, 4 * c + q + 1, act_lo)

            def chunk_taps(c):
                dve.tensor_copy(fw[:], fcw[:].rearrange("p k (g f) -> p k g f", g=2)[
                    :, :, :, bass.ds(4 * c, 4)]).then_inc(fw_ready, 1)
                dve.wait_ge(fw_ready, c + 1)

            chunk_taps(0)
            for q in range(4):
                gates((S_CHUNK0 + 4 * q, 0), q, 0, pair_banks(q, q == 0), q == 0)
                act_low(q, 0)
            with dve.Fori(1, CHUNKS - 1) as c:
                chunk_taps(c)
                gates((S_CHUNKS, c), 0, c, pair_banks(0))
                dve.wait_ge(res_ready, TT)
                add_out((S_CHUNKS + 4, c), c - 1 + HEADS // 2)
                act_low(0, c)
                for q in range(1, 4):
                    gates((S_CHUNKS + 8 + 4 * q, c), q, c, pair_banks(q))
                    act_low(q, c)
            chunk_taps(CHUNKS - 1)
            for q in range(4):
                gates((S_LAST_CHUNK + 4 * q, 0), q, CHUNKS - 1, pair_banks(q))
                act_low(q, CHUNKS - 1, mh2, ml2)

            def beside(n):
                for stage in beside_last(n):
                    split_low(stage)
            add_out((S_LAST_CHUNK + 16, 0), CHUNKS - 2 + HEADS // 2, False, beside)

            dve.wait_ge(gb_landed, 64)

            def gain(t, n):
                block_ = res[:, t, n * 512:(n + 1) * 512]
                dve.wait_ge(out_normed, 4 * t + n + 1)
                dve.tensor_tensor(block_, block_, gb[:, 2, n * 512:(n + 1) * 512], ALU.mult).then_inc(out_gained, 1)

            for t in range(TT):
                for n in range(NB):
                    block_ = res[:, t, n * 512:(n + 1) * 512]
                    dve.wait_ge(last_done, 4 * t + n + 1)
                    dve.tensor_tensor(block_, block_, ps[4 * ((t + 1) % 2) + n][:], ALU.add).then_inc(out_added, 1)
                    if t > 0:
                        gain(t - 1, n)
                    take_statistics(t, n, 16 * (CHUNKS - 1 + HEADS // 2) + 4 * t + n + 1)
                variance(t, 16 + 4 * t + 4)
                scaling(1, t)
            for n in range(NB):
                gain(TT - 1, n)
            for n in range(NB):
                if on_dve(TT - 1, n):
                    block_ = res[:, TT - 1, n * 512:(n + 1) * 512]
                    dve.wait_ge(out_gained, 4 * (TT - 1) + n + 1)
                    dve.tensor_tensor(block_, block_, gb[:, 3, n * 512:(n + 1) * 512],
                                      ALU.add).then_inc(out_ready_dve, 1)

        @block.gpsimd
        def _(pool):
            pool.wait_ge(xl_ready, 4 * TT)
            for t in range(TT):
                pool.tensor_scalar(res[:, t, :], res[:, t, :], ALPHA, None, ALU.mult).then_inc(x_scaled, 1)
            for k in range(1, KT, 2):
                pool.wait_ge(n_hi, k + 1)
                pool.tensor_tensor(xl[:, k, :], scr[:, 2 + k % 4, :], xh[:, k, :].bitcast(F32),
                                   ALU.subtract).then_inc(n_lo_pool, 1)
            pool.wait_ge(gb_landed, 64)
            pool.wait_ge(n_turned, KT)
            for t in range(TT):
                pool.tensor_tensor(res[:, t, :], res[:, t, :], gb[:, 0, :], ALU.mult).then_inc(res_step, 1)
                pool.wait_ge(res_step, 2 * t + 1)
                pool.tensor_tensor(res[:, t, :], res[:, t, :], gb[:, 1, :], ALU.add).then_inc(res_step, 1)
                pool.wait_ge(res_step, 2 * t + 2)
                pool.tensor_scalar(res[:, t, :], res[:, t, :], ALPHA, None, ALU.mult).then_inc(res_ready, 1)
            for t in range(TT):
                for n in range(NB):
                    if not on_dve(t, n):
                        block_ = res[:, t, n * 512:(n + 1) * 512]
                        pool.wait_ge(out_gained, 4 * t + n + 1)
                        pool.tensor_tensor(block_, block_, gb[:, 3, n * 512:(n + 1) * 512],
                                           ALU.add).then_inc(out_ready, 1)


INPUTS = ["x", "positions", "w_in", "q_norm_g", "w_uq", "kv_norm_g", "w_ukv", "conv_w", "w_out", "ln1_g",
          "ln1_b", "w_gate_up", "ffn_conv_w", "w_down", "ln2_g", "ln2_b"]


def kernel(**inputs):
    import concourse.bacc as bacc
    from concourse.bass_utils import run_bass_kernel_spmd

    nc = bacc.Bacc("TRN2", target_bir_lowering=False, num_devices=1, dynamic_dma_scratch_size=1024)
    arrays = {"in_consts": shape_constants()}
    for name in INPUTS:
        arrays[f"in_{name}"] = np.ascontiguousarray(inputs[name])
    args = [nc.dram_tensor(name, a.shape, mybir.dt.from_np(a.dtype), kind="ExternalInput").ap()
            for name, a in arrays.items()]
    out = nc.dram_tensor("out", (1, SEQ, D_MODEL), F32, kind="ExternalOutput").ap()
    hybrid_layer(nc, *args, out)
    r = run_bass_kernel_spmd(nc, [arrays], core_ids=[0])
    return r.results[0]["out"]
```

```python
import math
from contextlib import ExitStack

import numpy as np

import concourse.bass as bass
from concourse import mybir

ALU = mybir.AluOpType
ACT = mybir.ActivationFunctionType
AX_X = mybir.AxisListType.X
F32 = mybir.dt.float32
F32R = mybir.dt.float32r
I32 = mybir.dt.int32

P = 128
D_MODEL = 2048
SEQ = 512
HEADS = 8
NOPE = 128
ROPE = 64
HALF = ROPE // 2
VDIM = 128
Q_RANK = 512
KV_RANK = 256
CONV_WIDTH = D_MODEL - HEADS * VDIM
FFN = 5632
K = 3
LN_EPS = 1e-5
RMS_EPS = 1e-6
ALPHA = 2.0 ** 0.25
SCALE = float(NOPE + ROPE) ** -0.5
ROPE_THETA = 10000.0

KT = D_MODEL // P
TT = SEQ // P
NB = D_MODEL // 512
QT = Q_RANK // P
KVT = KV_RANK // P
FT = FFN // P
KV_COL = Q_RANK
KR_COL = Q_RANK + KV_RANK
B_COL = KR_COL + ROPE
C_COL = B_COL + CONV_WIDTH
X_COL = C_COL + CONV_WIDTH

PERIOD = 24
RAW = 4
SPLIT = 3
STAGE = 1024
S_KR = 2 * (QT + KVT)
S_ITER0 = S_KR + 2
S_HEADS = S_ITER0 + 16 - PERIOD
S_OUT_LAST = S_HEADS + PERIOD * (HEADS // 2)
S_CHUNK0 = S_OUT_LAST + 8
S_CHUNKS = S_CHUNK0 + 16 - PERIOD
BESIDE = [S_CHUNK0 + 1, S_CHUNK0 + 3]
CHUNKS = FT // 4
S_LAST_CHUNK = S_CHUNKS + PERIOD * (CHUNKS - 1)
S_DOWN_LAST = S_LAST_CHUNK + PERIOD
S_END = S_DOWN_LAST + 8
N_ANGLE = 17
assert PERIOD % RAW == 0 and PERIOD % SPLIT == 0

IT0 = [dict(c=0, ukv=2, uq=3, x=4, b=6), dict(c=8, ukv=10, uq=11, x=12, b=14)]
ITN = [dict(c=0, ukv=2, uq=3, out=4, x=12, b=14), dict(c=16, ukv=18, uq=19, x=20, b=22)]

G1, B1, CW, QG, KVG = 0, KT, 2 * KT, 2 * KT + K * 8, 2 * KT + K * 8 + QT
N_ROWS = KVG + KVT


def shape_constants():
    c = np.zeros((P, 2 * P + 1), np.float32)
    c[:, :P] = np.eye(P)
    c[:, P:2 * P] = np.where(np.arange(P)[None, :] <= np.arange(P)[:, None], 0.0, -1e30)
    freq = np.float64(ROPE_THETA) ** (-np.arange(0, ROPE, 2) / ROPE)
    c[:, 2 * P] = np.concatenate([freq, -freq] * 2).astype(np.float32)
    return c


def two_pi_parts():
    parts, rest = [], 2.0 * math.pi
    for _ in range(3):
        unit = 2.0 ** (math.floor(math.log2(rest)) - 10)
        parts.append(math.floor(rest / unit) * unit)
        rest -= parts[-1]
    return parts + [rest]


SHORT = {S_KR: 8 * ROPE, S_KR + 1: 8 * ROPE,
         S_ITER0 + IT0[1]["ukv"]: KVT * NOPE, S_ITER0 + IT0[1]["uq"]: QT * NOPE}
SHORT_LOOPED = {S_HEADS + ITN[1]["ukv"]: KVT * NOPE, S_HEADS + ITN[1]["uq"]: QT * NOPE}


def hybrid_layer(nc, consts, x, positions, w_in, q_norm_g, w_uq, kv_norm_g, w_ukv, conv_w, w_out,
                 ln1_g, ln1_b, w_gate_up, ffn_conv_w, w_down, ln2_g, ln2_b, out):
    with ExitStack() as ctx:
        def sb(name, shape, dt=F32, stack=ctx):
            return stack.enter_context(nc.sbuf_tensor(name, shape, dt))

        def sem(name):
            return ctx.enter_context(nc.semaphore(name))

        const = sb("const", [P, 2 * P + 1])
        ident, mask, freq = const[:, 0:P], const[:, P:2 * P], const[:, 2 * P:2 * P + 1]
        ones = sb("ones", [P, P])
        eps = sb("eps", [P, 2])
        vec = sb("vec", [P, N_ROWS])
        fcw = sb("fcw", [P, K, 2 * FT])
        fw = sb("fw", [P, K, 2, 4])
        cw = sb("cw", [P, K, 2])
        stat = sb("stat", [P, TT, NB, 6])
        mv = sb("mv", [P, TT, 2])
        std = sb("std", [P, TT])
        rstd = sb("rstd", [P, TT])
        shift = sb("shift", [P, TT])
        spare = sb("spare", [P, 1])
        mx = sb("mx", [P, TT])
        nmx = sb("nmx", [P, TT])
        psum_p = sb("psum_p", [P, TT])
        rsum = sb("rsum", [P, TT])
        res = sb("res", [P, TT, D_MODEL])
        xh = sb("xh", [P, KT, SEQ], F32R)
        xl = sb("xl", [P, KT, SEQ], F32R)
        mh = sb("mh", [P, 4, SEQ], F32R)
        ml = sb("ml", [P, 4, SEQ], F32R)
        scr = sb("scr", [P, 6, SEQ])
        raw = sb("raw", [P, RAW, STAGE])
        wh = sb("wh", [P, SPLIT, STAGE], F32R)
        wl = sb("wl", [P, SPLIT, STAGE], F32R)
        with ExitStack() as heads_only:
            cqh = sb("cqh", [P, QT, SEQ], F32R, heads_only)
            cql = sb("cql", [P, QT, SEQ], F32R, heads_only)
            ckh = sb("ckh", [P, KVT, SEQ], F32R, heads_only)
            ckl = sb("ckl", [P, KVT, SEQ], F32R, heads_only)
            krh = sb("krh", [P, SEQ], F32R, heads_only)
            krl = sb("krl", [P, SEQ], F32R, heads_only)
            cosines = sb("cosines", [P, SEQ], F32, heads_only)
            sines = sb("sines", [P, SEQ], F32, heads_only)
            att = sb("att", [P, 5 * SEQ], F32R, heads_only)
            qp1 = sb("qp1", [P, SEQ], F32R, heads_only)
            with ExitStack() as latents_only:
                sqs = sb("sqs", [P, 4, SEQ], F32, latents_only)
            vals = sb("vals", [P, 4, SEQ], F32R, heads_only)
        with ExitStack() as ffn_only:
            gb = sb("gb", [P, 4, D_MODEL], F32, ffn_only)
            mh2 = sb("mh2", [P, 4, SEQ], F32R, ffn_only)
            ml2 = sb("ml2", [P, 4, SEQ], F32R, ffn_only)
        wdh, wdl = (v[:].rearrange("p (s a) n -> p s (a n)", a=2) for v in (xh, xl))
        vh, vl = (vals[:, 2 * j:2 * j + 2, :].rearrange("p h (t n) -> p (h t) n", n=2 * VDIM) for j in range(2))
        qnh, qnl, knh, knl, qp0 = (att[:, j * SEQ:(j + 1) * SEQ] for j in range(5))
        qp = [qp0, qp1[:]]
        PT_OFF = [0, 512, 896, 1152, 1280]
        pth, ptl = att[:, 0:1280], att[:, 1280:2560]
        P_OFF = [0, 128, 384, 768, 1280]
        scr_flat = scr[:].rearrange("p a b -> p (a b)")
        prob = scr_flat[:, 0:1280]
        c_sb = scr_flat[:, 1280:1792]
        tmp_a = scr_flat[:, 1792:2304]
        tmp_b = scr_flat[:, 2304:2816]
        lat = [scr[:, j, :] for j in range(6)]
        rows = scr[:, 0, 0:P]
        frows = scr[:, 0, P:P + K * P].rearrange("p (k n) -> p k n", k=K)
        pos = scr[:, 1, :]
        ang, turns, turns_hi, turns_lo = (scr[:, j, :] for j in (2, 3, 4, 5))
        yg, yu, sg, a_f = (scr[:, j, :] for j in range(4))

        ps = [ctx.enter_context(nc.psum_tensor(f"bank{b}", [P, 512], F32)) for b in range(8)]
        B_LAT = [2, 3, 0, 1, 2, 3]
        B_KR, B_RMS = 4, [5, 6]
        B_C, B_PV, B_KN, B_QN, B_QR, B_X, B_B = 0, 1, 4, 6, 7, 4, 5
        B_V = [5, 2]
        B_PT = [6, 7, 4]
        B_LAST_PV = 5

        raw_landed = [sem(f"raw_landed{j}") for j in range(RAW)]
        x_landed = [sem(f"x_landed{t}") for t in range(TT)]
        (const_landed, rows_landed, pos_landed, rope_landed, gb_landed, out_written) = map(
            sem, ("const_landed", "rows_landed", "pos_landed", "rope_landed", "gb_landed", "out_written"))
        (stage_used, rows_turned, x_turned, rms_sum, score_done, pt_done, pv_done, out_done, n_turned,
         last_done) = map(
            sem, ("stage_used", "rows_turned", "x_turned", "rms_sum", "score_done", "pt_done", "pv_done",
                  "out_done", "n_turned", "last_done"))
        (split_hi, xh_ready, lat_squared, rms_root, lat_hi, cs_ready, kr_moved, kr_hi, c_copied, kn_hi, v_hi, qn_hi,
         qr_hi, exp_done, conv_hi, pt_hi, pv_hi, std_ready, normed_act, n_hi, g_scaled, u_scaled, silu_done,
         act_hi, out_normed) = map(
            sem, ("split_hi", "xh_ready", "lat_squared", "rms_root", "lat_hi", "cs_ready", "kr_moved", "kr_hi",
                  "c_copied", "kn_hi", "v_hi", "qn_hi", "qr_hi", "exp_done", "conv_hi", "pt_hi", "pv_hi",
                  "std_ready", "normed_act", "n_hi", "g_scaled", "u_scaled", "silu_done", "act_hi", "out_normed"))
        (split_lo, set_up, angle_step, vec_ready, xl_ready, sq_added, rms_inv, lat_normed, lat_lo,
         kr_summed, kr_prod, kr_rot, kr_lo) = map(
            sem, ("split_lo", "set_up", "angle_step", "vec_ready", "xl_ready", "sq_added", "rms_inv",
                  "lat_normed", "lat_lo", "kr_summed", "kr_prod", "kr_rot", "kr_lo"))
        (cw_ready, kn_lo, v_lo, qn_lo, qr_prod, qr_rot, qr_lo, x_used, conv_tap, b_used, conv_lo, masked,
         max_taken, max_ready, sum_inv, p_ready, pt_lo, pv_lo, out_added) = map(
            sem, ("cw_ready", "kn_lo", "v_lo", "qn_lo", "qr_prod", "qr_rot", "qr_lo", "x_used", "conv_tap",
                  "b_used", "conv_lo", "masked", "max_taken", "max_ready", "sum_inv", "p_ready", "pt_lo",
                  "pv_lo", "out_added"))
        (stats_taken, var_ready, rstd_ready, shift_ready, normed_dve, n_full, n_lo, fw_ready, g_tap, g_conv,
         u_tap, u_conv, act_full, act_lo, out_gained, out_ready_dve) = map(
            sem, ("stats_taken", "var_ready", "rstd_ready", "shift_ready", "normed_dve", "n_full", "n_lo",
                  "fw_ready", "g_tap", "g_conv", "u_tap", "u_conv", "act_full", "act_lo", "out_gained",
                  "out_ready_dve"))
        (x_scaled, n_lo_pool, res_step, res_ready, out_ready) = map(
            sem, ("x_scaled", "n_lo_pool", "res_step", "res_ready", "out_ready"))

        def ahead(stage, n):
            return (stage[0] + n, stage[1])

        def wait_stage(eng, s, stage, back=0):
            number, i = stage
            if number + 1 - back > 0:
                eng.wait_ge(s, number + 1 - back + PERIOD * i)

        def split_slot(stage, side_by_side=True):
            number, i = stage
            if isinstance(i, int) and number in (S_KR, S_KR + 1) and side_by_side:
                both = wh[:, number % SPLIT, :].rearrange("p (k n) -> p k n", n=2 * ROPE)
                return [both[:, :, 0:ROPE], both[:, :, ROPE:]]
            if isinstance(i, int) and number in BESIDE:
                a = 2 * BESIDE.index(number)
                return [v[:, a:a + 2, :].rearrange("p k n -> p (k n)") for v in (mh2, ml2)]
            if isinstance(i, int) and number >= S_DOWN_LAST:
                return [v[:, number - S_DOWN_LAST, :] for v in (wdh, wdl)]
            return [v[:, number % SPLIT, :] for v in (wh, wl)]

        def length(stage):
            number, i = stage
            return (SHORT if isinstance(i, int) else SHORT_LOOPED).get(number, STAGE)

        def splitting(stage):
            number, i = stage
            n = length(stage)
            loaded, (high, low) = raw[:, number % RAW, 0:n], split_slot(stage)
            if isinstance(i, int) and number in (S_KR, S_KR + 1):
                return loaded.rearrange("p (k n) -> p k n", n=ROPE), high, low
            return loaded, high[:, 0:n], low[:, 0:n]

        def split_high(stage):
            number, i = stage
            if isinstance(i, int) and number >= S_END:
                return
            act = nc.scalar
            act.wait_ge(raw_landed[number % RAW], 16 * (number // RAW + 1) + 16 * (PERIOD // RAW) * i)
            if isinstance(i, int) and number >= S_DOWN_LAST:
                wait_stage(act, stage_used, (S_DOWN_LAST - 9, 0))
            elif isinstance(i, int) and number in BESIDE:
                act.wait_ge(pv_done, HEADS)
            else:
                wait_stage(act, stage_used, stage, back=SPLIT)
            if number == (S_ITER0 + IT0[0]["uq"] if isinstance(i, int) else S_HEADS + ITN[0]["uq"]):
                act.wait_ge(rope_landed, 16 + 16 * i)
            as_loaded, high, _ = splitting(stage)
            act.copy(high, as_loaded).then_inc(split_hi, 1)

        def split_low(stage):
            number, i = stage
            if isinstance(i, int) and number >= S_END:
                return
            dve = nc.vector
            wait_stage(dve, split_hi, stage)
            as_loaded, high, low = splitting(stage)
            dve.tensor_tensor(low, as_loaded, high.bitcast(F32), ALU.subtract).then_inc(split_lo, 1)

        def pair_banks(q, crossed=False):
            return (0, 1) if crossed else (4 + 2 * (q % 2), 5 + 2 * (q % 2))

        def beside_last(n):
            first = S_LAST_CHUNK + 16
            if n < 5:
                return [(first + n + SPLIT, 0)]
            return [(S_DOWN_LAST + k, 0) for k in ((0, 1, 2), (3, 4, 5), (6, 7))[n - 5]]

        STEPS = 2 * KT
        turned = [ps[4 + j][:, 0:256] for j in range(4)]
        full = [scr[:, 2 + j // 2, (j % 2) * 256:(j % 2 + 1) * 256] for j in range(8)]
        LOW_ON_DVE = [0, 2]

        def low_made(step):
            before = sum(n < step for n in LOW_ON_DVE)
            return (n_lo, before + 1) if step in LOW_ON_DVE else (n_lo_pool, step + 1 - before)

        def part_of(v, step):
            return v[:, step % KT, step // KT * 256:(step // KT + 1) * 256]

        def on_dve(t, n):
            return t == TT - 1 and n >= 1

        block = ctx.enter_context(nc.Block())

        @block.sync
        def _(sp):
            w_in_t = w_in[0].rearrange("(h k p) n -> h p k n", h=2, p=P)
            w_uq_t = w_uq[0].rearrange("(k p) n -> p k n", p=P)
            w_ukv_t = w_ukv[0].rearrange("(k p) n -> p k n", p=P)
            w_out_t = w_out[0].rearrange("(g h p) n -> p g h n", g=2, p=P)
            w_gu_t = w_gate_up[0].rearrange("(h k p) n -> h p k n", h=2, p=P)
            w_down_t = w_down[0].rearrange("(k p) n -> p k n", p=P)

            def load(stage, rows_, start, count, source, row=None):
                number, i = stage
                row = row or count
                dst = raw[:, number % RAW, 0:rows_ * row].rearrange("p (k n) -> p k n", n=row)[:, :, 0:count]
                at = start if isinstance(start, int) else sp.snap(start)
                wait_stage(sp, split_lo, stage, back=RAW)
                sp.dma_start(dst, source(at)).then_inc(raw_landed[number % RAW], 16)

            def load_in(stage, column, width=P, halves=(0, 1)):
                for h in halves:
                    load(ahead(stage, h), 8, column, width, lambda at: w_in_t[h][:, :, bass.ds(at, width)])

            def load_out(stage, i):
                for n in range(NB):
                    for j in range(2):
                        load(ahead(stage, 2 * n + j), 2, 2 * i + j, 512, lambda at: w_out_t[
                            :, :, bass.ds(at, 1), n * 512:(n + 1) * 512].rearrange("p g h n -> p (g h) n"))

            def load_down(stage, c):
                for n in range(NB):
                    for j in range(2):
                        load(ahead(stage, 2 * n + j), 2, 4 * c + 2 * j, 512, lambda at: w_down_t[
                            :, bass.ds(at, 2), n * 512:(n + 1) * 512])

            def load_heads(base, i, table):
                for hh, at in enumerate(table):
                    head = 2 * i + hh
                    load_in(ahead(base, at["c"]), C_COL + P * head)
                    both = hh == 0
                    kv, q = (2 * (NOPE + VDIM), NOPE + ROPE) if both else (NOPE, NOPE)
                    load(ahead(base, at["ukv"]), KVT, 512 * i, kv,
                         lambda a: w_ukv_t[:, :, 256 * hh:][:, :, bass.ds(a, kv)])
                    load(ahead(base, at["uq"]), QT, 384 * i, q, lambda a: w_uq_t[:, :, 192 * hh:][:, :, bass.ds(a, q)],
                         NOPE + 2 * ROPE if both else NOPE)
                    if both:
                        slot = raw[:, (base[0] + at["uq"]) % RAW, :].rearrange("p (k n) -> p k n", k=QT)
                        sp.dma_start(slot[:, :, NOPE + ROPE:], w_uq_t[:, :, 192 + NOPE:][
                            :, :, bass.ds(384 * i, ROPE)]).then_inc(rope_landed, 16)
                    if "out" in at:
                        load_out(ahead(base, at["out"]), i - 1)
                    load_in(ahead(base, at["x"]), X_COL + P * head)
                    load_in(ahead(base, at["b"]), B_COL + P * head)

            def load_pair(stage, tile):
                for j in range(2):
                    for h in range(2):
                        load(ahead(stage, 2 * j + h), 8, j * FFN + P * tile, P,
                             lambda at: w_gu_t[h][:, :, bass.ds(at, P)])

            def load_crossed(stage, tile):
                for h in range(2):
                    for j in range(2):
                        load(ahead(stage, 2 * h + j), 8, j * FFN + P * tile, P,
                             lambda at: w_gu_t[h][:, :, bass.ds(at, P)])

            for t in range(TT):
                sp.dma_start(res[:, t, :], x[0, t * P:(t + 1) * P, :]).then_inc(x_landed[t], 16)
                if 1 <= t < 3:
                    load_in((0, 0), KV_COL, halves=(t - 1,))
            for at, v in ((G1, ln1_g[0].rearrange("(k p) -> k p", p=P)), (B1, ln1_b[0].rearrange("(k p) -> k p", p=P)),
                          (CW, conv_w[0].rearrange("k (h p) -> (k h) p", p=P)),
                          (QG, q_norm_g[0].rearrange("(k p) -> k p", p=P)),
                          (KVG, kv_norm_g[0].rearrange("(k p) -> k p", p=P))):
                sp.dma_start(rows[at:at + v.shape[0], :], v).then_inc(rows_landed, 16)
            sp.dma_start(frows[0:2 * FT], ffn_conv_w[0].rearrange("k (r p) -> r k p", p=P)).then_inc(rows_landed, 16)
            sp.dma_start(pos.bitcast(I32), positions[0].partition_broadcast(P)).then_inc(pos_landed, 16)
            load_in((2, 0), KV_COL + P)
            for j in range(QT):
                load_in((4 + 2 * j, 0), j * P)
            load_in((12, 0), KR_COL, ROPE)
            load_heads((S_ITER0, 0), 0, IT0)
            with sp.Fori(1, HEADS // 2) as i:
                load_heads((S_HEADS, i), i, ITN)
            load_out((S_OUT_LAST, 0), HEADS // 2 - 1)
            load_crossed((S_CHUNK0, 0), 0)
            for q in range(1, 3):
                load_pair((S_CHUNK0 + 4 * q, 0), q)
            sp.wait_ge(pv_done, HEADS)
            for j, v in enumerate((ln1_g, ln1_b, ln2_g, ln2_b)):
                sp.dma_start(gb[:, j, :], v[0].partition_broadcast(P)).then_inc(gb_landed, 16)
            load_pair((S_CHUNK0 + 12, 0), 3)
            with sp.Fori(1, CHUNKS - 1) as c:
                load_pair((S_CHUNKS, c), 4 * c)
                load_down((S_CHUNKS + 4, c), c - 1)
                for q in range(1, 4):
                    load_pair((S_CHUNKS + 8 + 4 * q, c), 4 * c + q)
            for q in range(4):
                load_pair((S_LAST_CHUNK + 4 * q, 0), 4 * (CHUNKS - 1) + q)
            load_down((S_LAST_CHUNK + 16, 0), CHUNKS - 2)
            load_down((S_DOWN_LAST, 0), CHUNKS - 1)
            for t in range(TT):
                for n in sorted(range(NB), key=lambda n: not on_dve(t, n)):
                    if on_dve(t, n):
                        sp.wait_ge(out_ready_dve, n)
                    else:
                        sp.wait_ge(out_ready, 4 * t + n + 1)
                    cols = slice(n * 512, (n + 1) * 512)
                    sp.dma_start(out[0, t * P:(t + 1) * P, cols], res[:, t, cols]).then_inc(out_written, 16)
            sp.wait_ge(out_written, 16 * TT * NB)

        @block.tensor
        def _(pe):
            def pieces3(stage, width):
                return [v.rearrange("p (k n) -> p k n", n=width)
                        for v in split_slot(stage)]

            def products(dst, pairs):
                for n, (sh, sl, vh_, vl_) in enumerate(pairs):
                    pe.matmul(dst, sh, vh_, start=(n == 0), stop=False)
                    pe.matmul(dst, sl, vh_, start=False, stop=False)
                    last = pe.matmul(dst, sh, vl_, start=False, stop=(n == len(pairs) - 1))
                return last

            def channels(w3, half, bank, cols=slice(0, SEQ), before=None):
                w3h, w3l = w3
                for k in range(8):
                    kk = 8 * half + k
                    if before:
                        before(kk)
                    for j, (w, v) in enumerate(((w3h, xh), (w3l, xh), (w3h, xl))):
                        last = pe.matmul(ps[bank][:, cols], w[:, k, :], v[:, kk, cols],
                                         start=(kk == 0 and j == 0), stop=(kk == KT - 1 and j == 2))
                return last

            def project(stage, bank):
                for half in range(2):
                    wait_stage(pe, split_lo, ahead(stage, half))
                    channels(pieces3(ahead(stage, half), P), half, bank).then_inc(stage_used, 1)

            def rows_of_out(t, slots, w3, before=lambda t, slot: None):
                tok = slice(t * P, (t + 1) * P)
                w3h, w3l = w3
                for slot in slots:
                    before(t, slot)
                    for q, (v, w) in enumerate(((mh, w3h), (ml, w3h), (mh, w3l))):
                        last = pe.matmul(ps[t][:], v[:, slot, tok], w[:, slot % 2, :],
                                         start=(slot == 0 and q == 0), stop=(slot == 2 and q == 2))
                return last

            SLOTS = ((0, 1), (3, 2))

            def project_out(stage, m, before, blocks=NB):
                for n in range(blocks):
                    for j in range(2):
                        st = ahead(stage, 2 * n + j)
                        wait_stage(pe, split_lo, st)
                        for t in range(TT):
                            if j == 0 and n > 0:
                                pe.wait_ge(out_added, 16 * m + 4 * (n - 1) + t + 1)
                            last = rows_of_out(t, SLOTS[j], pieces3(st, 512), *([before] if n == 0 else []))
                            if j == 1 and t < TT - 1:
                                last.then_inc(out_done, 1)
                        last.then_inc(stage_used, 1)

            pe.wait_ge(const_landed, 16)
            for t in range(TT):
                pe.wait_ge(x_landed[t], 16)
                for g in range(4):
                    if t > 0:
                        pe.wait_ge(xl_ready, 4 * (t - 1) + g + 1)
                    for k in range(4):
                        last = pe.transpose(ps[4 + g][:, k * P:(k + 1) * P],
                                            res[:, t, (4 * g + k) * P:(4 * g + k + 1) * P], ident)
                    last.then_inc(x_turned, 1)
                if t >= 2:
                    half = t - 2
                    wait_stage(pe, split_lo, (half, 0))
                    channels(pieces3((half, 0), P), half, B_LAT[0], slice(0, SEQ // 2))
            for half in range(2):
                channels(pieces3((half, 0), P), half, B_LAT[0], slice(SEQ // 2, SEQ),
                         lambda kk: pe.wait_ge(xl_ready, 4 * (TT - 1) + kk // 4 + 1)).then_inc(stage_used, 1)
            pe.wait_ge(rows_landed, 16 * 6)
            last = pe.transpose(ps[0][:, 0:N_ROWS], rows[0:N_ROWS, :], ident[0:N_ROWS, 0:N_ROWS])
            last.then_inc(rows_turned, 1)
            for k in range(K):
                last = pe.transpose(ps[1][:, k * 2 * FT:(k + 1) * 2 * FT], frows[0:2 * FT, k, :],
                                    ident[0:2 * FT, 0:2 * FT])
            last.then_inc(rows_turned, 1)
            for j in range(1, KVT + QT):
                if j == 2:
                    pe.wait_ge(vec_ready, 2)
                if j >= 4:
                    pe.wait_ge(lat_squared, j - 3)
                project((2 * j, 0), B_LAT[j])
                if j == 2:
                    pe.wait_ge(sq_added, 1)
                    pe.matmul(ps[B_RMS[0]][:], ones[:], sqs[:, 2, :], start=True, stop=True).then_inc(rms_sum, 1)
            for half in range(2):
                wait_stage(pe, split_lo, (S_KR + half, 0))
                both = split_slot((S_KR + half, 0), False)[0].rearrange("p (k n) -> p k n", n=2 * ROPE)
                for k in range(8):
                    kk = 8 * half + k
                    for v, w in (((xh, 2 * ROPE), (xl, ROPE)) if kk < KT - 1 else ((xl, ROPE), (xh, 2 * ROPE))):
                        last = pe.matmul(ps[B_KR][0:w, :], both[:, k, 0:w], v[:, kk, :], start=(kk == 0 and w > ROPE),
                                         stop=(kk == KT - 1 and w > ROPE))
                last.then_inc(stage_used, 1)
                if half == 0:
                    pe.wait_ge(sq_added, 4)
                    pe.matmul(ps[B_RMS[1]][:], ones[:], sqs[:, 3, :], start=True, stop=True).then_inc(rms_sum, 1)

            def values(head, hh, bank=B_PV):
                n = 0
                for j in range(TT):
                    pe.wait_ge(pt_lo, 3 * head + min(j, 2) + 1)
                    cols = slice(PT_OFF[j], PT_OFF[j + 1])
                    for v, p in ((vh, pth), (vl, pth), (vh, ptl)):
                        last = pe.matmul(ps[bank][:, j * P:512], v[:, j, hh * VDIM:(hh + 1) * VDIM], p[:, cols],
                                         start=(n == 0), stop=(n == 11))
                        n += 1
                last.then_inc(pv_done, 1)

            def heads(base, i, table, first):
                for hh, at in enumerate(table):
                    head = 2 * i + hh
                    project(ahead(base, at["c"]), B_C)
                    if not (first and hh == 0):
                        values(head - 1, 1 - hh)
                    st = ahead(base, at["ukv"])
                    wait_stage(pe, split_lo, st)
                    if first and hh == 0:
                        pe.wait_ge(lat_lo, KVT)
                        pe.wait_ge(kr_summed, 1)
                    else:
                        pe.wait_ge(b_used, head)
                    w3h, w3l = pieces3(st, 2 * (NOPE + VDIM) if hh == 0 else NOPE)
                    last = products(ps[B_KN][:], [(w3h[:, k, 0:NOPE], w3l[:, k, 0:NOPE], ckh[:, k, :], ckl[:, k, :])
                                                  for k in range(KVT)])
                    if hh == 0:
                        if first:
                            pe.wait_ge(lat_squared, KVT + QT)
                        else:
                            pe.wait_ge(exp_done, 4 * head)
                        w4h, w4l = (w.rearrange("p k (h n) -> p k h n", h=2)[:, :, :, NOPE:] for w in (w3h, w3l))
                        for t in range(TT):
                            tok = slice(t * P, (t + 1) * P)
                            dst = ps[B_V[t // 2]][:, (t % 2) * 256:(t % 2 + 1) * 256].rearrange("p (h n) -> p h n", h=2)
                            last = products(dst, [(ckh[:, k, tok], ckl[:, k, tok], w4h[:, k], w4l[:, k])
                                                  for k in range(KVT)])
                    last.then_inc(stage_used, 1)
                    st = ahead(base, at["uq"])
                    wait_stage(pe, split_lo, st)
                    if first and hh == 0:
                        pe.wait_ge(lat_lo, KVT + QT)
                    w3h, w3l = pieces3(st, NOPE + 2 * ROPE if hh == 0 else NOPE)
                    for bank, a in ((B_QN, 0), (B_QR, NOPE))[0:2 - hh]:
                        last = products(ps[bank][:], [
                            (w3h[:, k, a:a + P], w3l[:, k, a:a + P], cqh[:, k, :], cql[:, k, :]) for k in range(QT)])
                    last.then_inc(stage_used, 1)
                    if "out" in at:
                        def before(t, slot):
                            if (t, slot) == (0, 0):
                                pe.wait_ge(v_lo, 2 * i + 2)
                                pe.wait_ge(c_copied, head + 1)
                                pe.wait_ge(pv_lo, 2 * i)
                                pe.wait_ge(conv_lo, 2 * i)
                        project_out(ahead(base, at["out"]), i - 1, before)
                    pe.wait_ge(kn_lo, head + 1)
                    project(ahead(base, at["x"]), B_X)
                    pe.wait_ge(v_lo, 2 * i + 2)
                    pe.wait_ge(qn_lo, head + 1)
                    pe.wait_ge(qr_lo, head + 1)
                    if first and hh == 0:
                        pe.wait_ge(kr_lo, 1)
                    if "out" in at:
                        pe.wait_ge(out_added, 16 * i)
                    else:
                        pe.wait_ge(c_copied, head + 1)
                        if not (first and hh == 0):
                            pe.wait_ge(pv_lo, head)
                    for j in range(TT):
                        tok, keys = slice(j * P, (j + 1) * P), slice(0, (j + 1) * P)
                        for n, (a, b) in enumerate(((qnh, knh), (qnl, knh), (qnh, knl), (qp[hh], krh), (qp[hh], krl))):
                            last = pe.matmul(ps[j][:, keys], a[:, tok], b[:, keys], start=(n == 0), stop=(n == 4))
                        last.then_inc(score_done, 1)
                    project(ahead(base, at["b"]), B_B)
                    pe.wait_ge(x_used, head + 1)
                    pe.wait_ge(p_ready, 4 * head + 4)
                    for n, tiles in enumerate(((0,), (1,), (2, 3))):
                        for j in tiles:
                            for q in range(j, TT):
                                to = PT_OFF[j] - PT_OFF[tiles[0]] + (q - j) * P
                                last = pe.transpose(ps[B_PT[n]][:, to:to + P],
                                                    prob[:, P_OFF[q] + j * P:P_OFF[q] + (j + 1) * P], ident)
                        last.then_inc(pt_done, 1)

            heads((S_ITER0, 0), 0, IT0, True)
            with pe.Fori(1, HEADS // 2) as i:
                heads((S_HEADS, i), i, ITN, False)

            def before_last(t, slot):
                if (t, slot) == (0, 0):
                    pe.wait_ge(pv_lo, HEADS - 1)
                    pe.wait_ge(conv_lo, HEADS - 1)
                elif (t, slot) == (TT - 1, 0):
                    values(HEADS - 1, 1, B_LAST_PV)
                elif (t, slot) == (0, 3):
                    pe.wait_ge(conv_lo, HEADS)
                elif (t, slot) == (0, 2):
                    pe.wait_ge(pv_lo, HEADS)

            project_out((S_OUT_LAST, 0), HEADS // 2 - 1, before_last, NB - 1)
            for j in range(2):
                wait_stage(pe, split_lo, (S_CHUNK0 - 2 + j, 0))
            for t in range(TT):
                pe.wait_ge(out_added, 16 * (HEADS // 2 - 1) + 4 * (NB - 2) + t + 1)
                for j in range(2):
                    last = rows_of_out(t, SLOTS[j], pieces3((S_CHUNK0 - 2 + j, 0), 512))
                    if j == 1 or t == TT - 1:
                        last.then_inc(out_done if t < TT - 1 else stage_used, 1)

            def turn(g):
                half, n = g // 4, g % 4
                if n == 0:
                    pe.wait_ge(normed_dve, 2 * half + 2)
                else:
                    pe.wait_ge(normed_act, 6 + 2 * n if half else 3 + n)
                for step in range(4 * g, 4 * g + 4):
                    if step >= 4:
                        pe.wait_ge(n_full, step - 3)
                    for j in range(2):
                        k = step % KT
                        last = pe.transpose(turned[step % 4][:, j * P:(j + 1) * P],
                                            res[:, 2 * half + j, k * P:(k + 1) * P], ident)
                    last.then_inc(n_turned, 1)

            def crossed_pair(stage):
                pe.wait_ge(out_added, 16 * (HEADS // 2 - 1) + 4 * (NB - 1) + 2)
                turn(0)
                for step in range(STEPS):
                    h, k = step % KT // 8, step % 8
                    if step % 4 == 2 and step + 2 < STEPS:
                        turn(step // 4 + 1)
                    if k == 0:
                        for j in range(2):
                            wait_stage(pe, split_lo, ahead(stage, 2 * h + j))
                    pe.wait_ge(*low_made(step))
                    for j in range(2):
                        w3h, w3l = pieces3(ahead(stage, 2 * h + j), P)
                        dst = ps[j][:, step // KT * 256:(step // KT + 1) * 256]
                        for q, (w, v) in enumerate(((w3h, xh), (w3l, xh), (w3h, xl))):
                            last = pe.matmul(dst, w[:, k, :], part_of(v, step),
                                             start=(step % KT == 0 and q == 0),
                                             stop=(step % KT == KT - 1 and q == 2))
                        if step >= KT and k == 7:
                            last.then_inc(stage_used, 1)

            def pair(stage, q, c, first):
                for j, free in enumerate((g_conv, u_conv)):
                    if first and q < 3:
                        pe.wait_ge(n_full, STEPS)
                    else:
                        pe.wait_ge(free, 4 * c + q - 1)
                    project(ahead(stage, 2 * j), pair_banks(q)[j])

            def down(stage, c):
                def before(t, slot):
                    if (t, slot) == (0, 0):
                        pe.wait_ge(out_added, 16 * (c + HEADS // 2))
                        pe.wait_ge(act_lo, 4 * c + 2)
                    elif (t, slot) == (0, 3):
                        pe.wait_ge(act_lo, 4 * c + 4)
                project_out(stage, c + HEADS // 2, before)

            crossed_pair((S_CHUNK0, 0))
            for q in range(1, 4):
                pair((S_CHUNK0 + 4 * q, 0), q, 0, True)
            with pe.Fori(1, CHUNKS - 1) as c:
                pair((S_CHUNKS, c), 0, c, False)
                down((S_CHUNKS + 4, c), c - 1)
                for q in range(1, 4):
                    pair((S_CHUNKS + 8 + 4 * q, c), q, c, False)
            for q in range(4):
                pair((S_LAST_CHUNK + 4 * q, 0), q, CHUNKS - 1, False)
            down((S_LAST_CHUNK + 16, 0), CHUNKS - 2)
            for t in range(TT):
                tok = slice(t * P, (t + 1) * P)
                for n in range(NB):
                    bank = 4 * ((t + 1) % 2) + n
                    if t == 0:
                        pe.wait_ge(g_conv, FT)
                        pe.wait_ge(u_conv, FT)
                        pe.wait_ge(act_lo, FT)
                    else:
                        m = CHUNKS - 2 + HEADS // 2 if t == 1 else CHUNKS - 1 + HEADS // 2
                        pe.wait_ge(out_added, 16 * m + (12 if t == 1 else 4 * (t - 2)) + n + 1)
                    for k in range(4):
                        if t == 0 and k % 2 == 0:
                            wait_stage(pe, split_lo, (S_DOWN_LAST + 2 * n + k // 2, 0))
                        w3h, w3l = (w[:, 2 * n + k // 2, (k % 2) * 512:(k % 2 + 1) * 512] for w in (wdh, wdl))
                        for q, (v, w) in enumerate(((mh2, w3h), (ml2, w3h), (mh2, w3l))):
                            last = pe.matmul(ps[bank][:], v[:, k, tok], w, start=(k == 0 and q == 0),
                                             stop=(k == 3 and q == 2))
                    last.then_inc(last_done, 1)

        @block.scalar
        def _(act):
            def after(stage):
                split_high(ahead(stage, SPLIT))

            act.dma_start(const[:], consts).then_inc(const_landed, 16)
            act.wait_ge(set_up, 1)
            act.copy(spare[:], eps[:, 0:1])
            for t in range(TT):
                for g in range(4):
                    act.wait_ge(x_turned, 4 * t + g + 1)
                    act.copy(xh[:, 4 * g:4 * g + 4, t * P:(t + 1) * P],
                             ps[4 + g][:].rearrange("p (k n) -> p k n", n=P)).then_inc(xh_ready, 1)
                if 1 <= t < 3:
                    split_high((t - 1, 0))
            split_high((2, 0))

            def latent(j):
                act.copy(lat[j], ps[B_LAT[j]][:])
                if j >= 2:
                    act.wait_ge(sq_added, 1 if j < 4 else 2)
                act.activation(sqs[:, j % 2, :], ps[B_LAT[j]][:], ACT.Square).then_inc(lat_squared, 1)

            def root(n, rank, dst):
                act.wait_ge(rms_sum, n + 1)
                act.activation(dst, ps[B_RMS[n]][:], ACT.Sqrt, bias=eps[:, 1:2], scale=1.0 / rank).then_inc(rms_root, 1)

            for s in range(2 * (KVT + QT)):
                wait_stage(act, stage_used, (s, 0))
                if s == 1:
                    act.wait_ge(rows_turned, 2)
                if s == 3:
                    act.wait_ge(angle_step, N_ANGLE)
                    act.activation(cosines[:], turns, ACT.Sin)
                    act.activation(sines[:], ang, ACT.Sin).then_inc(cs_ready, 1)
                if s == 5:
                    act.wait_ge(cs_ready, 1)
                if s % 2 == 1:
                    latent(s // 2)
                after((s, 0))
                if s == 5:
                    root(0, KV_RANK, sqs[:, 2, :])
                    for k in range(KVT):
                        act.wait_ge(lat_normed, k + 1)
                        act.copy(ckh[:, k, :], lat[k]).then_inc(lat_hi, 1)
            after((S_KR, 0))
            root(1, Q_RANK, sqs[:, 3, :])
            for k in range(QT):
                act.wait_ge(lat_normed, KVT + k + 1)
                act.copy(cqh[:, k, :], lat[KVT + k]).then_inc(lat_hi, 1)
            after((S_KR + 1, 0))
            act.copy(sqs[0:ROPE, 1, :], ps[B_KR][ROPE:P, :]).then_inc(kr_moved, 1)
            act.wait_ge(kr_rot, 1)
            act.copy(krh[0:ROPE, :], sqs[0:ROPE, 2, :])
            act.copy(krh[ROPE:P, :], sqs[0:ROPE, 2, :]).then_inc(kr_hi, 1)

            def values_high(head, slot):
                act.wait_ge(pv_done, head + 1)
                act.copy(mh[:, slot, :], ps[B_PV][:]).then_inc(pv_hi, 1)

            def heads(base, i, table, first):
                for hh, at in enumerate(table):
                    head = 2 * i + hh

                    def st(name, n=0):
                        return ahead(base, at[name] + n)
                    after(st("c"))
                    wait_stage(act, stage_used, st("c", 1))
                    act.copy(c_sb, ps[B_C][:]).then_inc(c_copied, 1)
                    after(st("c", 1))
                    if not (first and hh == 0):
                        values_high(head - 1, 2 * (1 - hh))
                    wait_stage(act, stage_used, st("ukv"))
                    act.copy(knh, ps[B_KN][:]).then_inc(kn_hi, 1)
                    if hh == 0:
                        if first:
                            act.wait_ge(kr_lo, 1)
                        for n in range(2):
                            act.copy(vals[:, n, :], ps[B_V[n]][:]).then_inc(v_hi, 1)
                    after(st("ukv"))
                    wait_stage(act, stage_used, st("uq"))
                    act.copy(qnh, ps[B_QN][:]).then_inc(qn_hi, 1)
                    if hh == 0:
                        for n in range(2):
                            act.wait_ge(qr_rot, head + n + 1)
                            act.copy(qp[n][0:ROPE, :], (tmp_a, tmp_b)[n][0:ROPE, :]).then_inc(qr_hi, 1)
                    after(st("uq"))
                    if "out" in at:
                        for n in range(2 * NB):
                            after(st("out", n))
                    after(st("x"))
                    after(st("x", 1))
                    act.wait_ge(max_ready, head + 1)
                    for j in range(TT):
                        act.activation(prob[:, P_OFF[j]:P_OFF[j + 1]], ps[j][:, 0:(j + 1) * P], ACT.Exp,
                                       bias=nmx[:, j:j + 1], scale=SCALE,
                                       accum_out=psum_p[:, j:j + 1]).then_inc(exp_done, 1)
                    after(st("b"))
                    act.wait_ge(b_used, head + 1)
                    act.copy(mh[:, 2 * hh + 1, :], tmp_a).then_inc(conv_hi, 1)
                    after(st("b", 1))
                    for n in range(3):
                        act.wait_ge(pt_done, 3 * head + n + 1)
                        a, b = PT_OFF[n], PT_OFF[n + 1 if n < 2 else 4]
                        act.copy(pth[:, a:b], ps[B_PT[n]][:, 0:b - a]).then_inc(pt_hi, 1)

            heads((S_ITER0, 0), 0, IT0, True)
            with act.Fori(1, HEADS // 2) as i:
                heads((S_HEADS, i), i, ITN, False)
            act.wait_ge(pv_done, HEADS)
            act.copy(mh[:, 2, :], ps[B_LAST_PV][:]).then_inc(pv_hi, 1)
            for n in range(2 * NB - 2):
                after((S_OUT_LAST + n, 0))
            split_high((S_CHUNK0 + 1, 0))

            def deviation(n, t):
                act.wait_ge(var_ready, TT * n + t + 1)
                act.activation(std[:, t:t + 1], mv[:, t, 1:2], ACT.Sqrt, bias=eps[:, 0:1]).then_inc(std_ready, 1)

            def normalise(t, n, s):
                block_ = res[:, t, n * 512:(n + 1) * 512]
                act.activation(block_, block_, ACT.Identity, bias=shift[:, t:t + 1],
                               scale=rstd[:, t:t + 1]).then_inc(s, 1)

            act.activation(spare[:], eps[:, 0:1], ACT.Sqrt)

            def norm_high(first, end):
                for step in range(first, end):
                    act.wait_ge(n_full, step + 1)
                    act.copy(part_of(xh, step), full[step % 8]).then_inc(n_hi, 1)

            def other_block(t, n):
                act.wait_ge(shift_ready, t + 1)
                normalise(t, n, normed_act)

            for t in range(2):
                deviation(0, t)
                for n in range(1, NB):
                    other_block(t, n)
            norm_high(0, 4)
            split_high((S_CHUNK0 + 2, 0))
            norm_high(4, 6)
            split_high((S_CHUNK0 + 3, 0))
            norm_high(6, 10)
            deviation(0, 2)
            norm_high(10, 12)
            other_block(2, 1)
            deviation(0, 3)
            norm_high(12, 16)
            other_block(3, 1)
            norm_high(16, 18)
            other_block(2, 2)
            other_block(3, 2)
            norm_high(18, 20)
            other_block(2, 3)
            other_block(3, 3)
            norm_high(20, STEPS)

            def gates(stage, q, c, banks, crossed=False):
                g_end = 2 if crossed else 1
                for n in range(1 if crossed else 0, g_end):
                    after(ahead(stage, n))
                wait_stage(act, stage_used, ahead(stage, g_end))
                act.wait_ge(fw_ready, c + 1)
                act.activation(yg, ps[banks[0]][:], ACT.Copy, scale=fw[:, K - 1, 0, q:q + 1]).then_inc(g_scaled, 1)
                for n in range(g_end, 3):
                    after(ahead(stage, n))
                wait_stage(act, stage_used, ahead(stage, 3))
                act.activation(yu, ps[banks[1]][:], ACT.Copy, scale=fw[:, K - 1, 1, q:q + 1]).then_inc(u_scaled, 1)
                act.wait_ge(g_conv, 4 * c + q + 1)
                act.activation(sg, yg, ACT.Silu).then_inc(silu_done, 1)
                after(ahead(stage, 3))

            def act_high(q, c, dst=mh):
                act.wait_ge(act_full, 4 * c + q + 1)
                act.copy(dst[:, q, :], a_f).then_inc(act_hi, 1)

            for q in range(4):
                gates((S_CHUNK0 + 4 * q, 0), q, 0, pair_banks(q, q == 0), q == 0)
                act_high(q, 0)
            with act.Fori(1, CHUNKS - 1) as c:
                gates((S_CHUNKS, c), 0, c, pair_banks(0))
                for n in range(2 * NB):
                    after((S_CHUNKS + 4 + n, c))
                act_high(0, c)
                for q in range(1, 4):
                    gates((S_CHUNKS + 8 + 4 * q, c), q, c, pair_banks(q))
                    act_high(q, c)
            for q in range(4):
                gates((S_LAST_CHUNK + 4 * q, 0), q, CHUNKS - 1, pair_banks(q))
                act_high(q, CHUNKS - 1, mh2)
            for n in range(2 * NB):
                for stage in beside_last(n):
                    split_high(stage)
            act.activation(spare[:], eps[:, 0:1], ACT.Sqrt)
            for t in range(TT):
                deviation(1, t)
                act.wait_ge(shift_ready, TT + t + 1)
                for n in range(NB):
                    if not on_dve(t, n):
                        normalise(t, n, out_normed)

        @block.vector
        def _(dve):
            def after(stage):
                split_low(ahead(stage, SPLIT))

            dve.memset(eps[:, 0:1], LN_EPS)
            dve.memset(eps[:, 1:2], RMS_EPS)
            dve.memset(ones[:], 1.0)
            dve.memset(krl[ROPE:P, :].bitcast(F32), 0.0).then_inc(set_up, 1)
            for t in range(TT):
                for g in range(4):
                    dve.wait_ge(xh_ready, 4 * t + g + 1)
                    four = (slice(None), slice(4 * g, 4 * g + 4), slice(t * P, (t + 1) * P))
                    dve.tensor_tensor(xl[four], ps[4 + g][:].rearrange("p (k n) -> p k n", n=P),
                                      xh[four].bitcast(F32), ALU.subtract).then_inc(xl_ready, 1)
                if 1 <= t < 3:
                    split_low((t - 1, 0))
            split_low((2, 0))

            angle_steps = [0]

            def step(ins):
                angle_steps[0] += 1
                ins.then_inc(angle_step, 1)
                dve.wait_ge(angle_step, angle_steps[0])

            def angles(part):
                if part == 0:
                    dve.wait_ge(pos_landed, 16)
                    step(dve.tensor_copy(ang, pos.bitcast(I32)))
                    step(dve.tensor_scalar(ang, ang, freq, None, ALU.mult))
                    step(dve.tensor_scalar(turns, ang, 1.0 / (2.0 * math.pi), 1.5 * 2.0 ** 23, ALU.mult, ALU.add))
                    step(dve.tensor_scalar(turns, turns, -1.5 * 2.0 ** 23, None, ALU.add))
                    step(dve.tensor_scalar(turns_hi, turns, 1.5 * 2.0 ** 34, None, ALU.add))
                    step(dve.tensor_scalar(turns_hi, turns_hi, -1.5 * 2.0 ** 34, None, ALU.add))
                    step(dve.tensor_tensor(turns_lo, turns, turns_hi, ALU.subtract))
                elif part == 1:
                    parts = two_pi_parts()
                    for size, counts in ((parts[0], (turns_hi, turns_lo)), (parts[1], (turns_hi, turns_lo)),
                                         (parts[2], (turns_hi, turns_lo)), (parts[3], (turns,))):
                        for n in counts:
                            step(dve.scalar_tensor_tensor(ang, n, -size, ang, ALU.mult, ALU.add))
                else:
                    step(dve.tensor_scalar(ang, ang, math.pi, -math.pi, ALU.min, ALU.max))
                    step(dve.scalar_tensor_tensor(turns, ang, -1.0, ang, ALU.mult, ALU.max))
                    step(dve.tensor_scalar(turns, turns, -1.0, math.pi / 2, ALU.mult, ALU.add))
                    assert angle_steps[0] == N_ANGLE, angle_steps

            def norm_latents(n, first, tiles, gain, high, low):
                inv = sqs[:, 2 + n, :]
                dve.wait_ge(rms_root, n + 1)
                dve.reciprocal(inv, inv).then_inc(rms_inv, 1)
                dve.wait_ge(rms_inv, n + 1)
                dve.wait_ge(vec_ready, 1)
                for k in range(tiles):
                    dve.scalar_tensor_tensor(lat[first + k], lat[first + k], vec[:, gain + k:gain + k + 1], inv,
                                             ALU.mult, ALU.mult).then_inc(lat_normed, 1)
                for k in range(tiles):
                    dve.wait_ge(lat_hi, first + k + 1)
                    dve.tensor_tensor(low[:, k, :], lat[first + k], high[:, k, :].bitcast(F32),
                                      ALU.subtract).then_inc(lat_lo, 1)

            for s in range(2 * (KVT + QT)):
                after((s, 0))
                if s < 3:
                    angles(s)
                if s == 1:
                    dve.wait_ge(rows_turned, 1)
                    dve.tensor_copy(vec[:], ps[0][:, 0:N_ROWS]).then_inc(vec_ready, 1)
                    dve.wait_ge(rows_turned, 2)
                    dve.tensor_copy(fcw[:].rearrange("p k n -> p (k n)"), ps[1][:, 0:K * 2 * FT]).then_inc(vec_ready, 1)
                if s % 2 == 1:
                    j = s // 2
                    dve.wait_ge(lat_squared, j + 1)
                    if j == 1:
                        dve.tensor_tensor(sqs[:, 2, :], sqs[:, 0, :], sqs[:, 1, :], ALU.add).then_inc(sq_added, 1)
                    if j == 3:
                        dve.tensor_tensor(sqs[:, 3, :], sqs[:, 0, :], sqs[:, 1, :], ALU.add).then_inc(sq_added, 1)
                    if j > 3:
                        dve.wait_ge(sq_added, j - 2)
                        dve.tensor_tensor(sqs[:, 3, :], sqs[:, 3, :], sqs[:, j % 2, :], ALU.add).then_inc(sq_added, 1)
                if s == 5:
                    norm_latents(0, 0, KVT, KVG, ckh, ckl)
            after((S_KR, 0))
            norm_latents(1, KVT, QT, QG, cqh, cql)
            after((S_KR + 1, 0))

            def rotate(source, n, dst, crossed, products_):
                dve.tensor_tensor(dst[0:n * ROPE, :], source[0:n * ROPE, :], cosines[0:n * ROPE, :],
                                  ALU.mult).then_inc(products_, 1)
                for half in range(2 * n):
                    here, there = (slice(h * HALF, (h + 1) * HALF) for h in (half, half ^ 1))
                    dve.tensor_tensor(crossed[there, :], source[here, :], sines[here, :],
                                      ALU.mult).then_inc(products_, 1)

            dve.wait_ge(cs_ready, 1)
            dve.wait_ge(kr_moved, 1)
            dve.tensor_tensor(sqs[0:ROPE, 0, :], ps[B_KR][0:ROPE, :], sqs[0:ROPE, 1, :], ALU.add).then_inc(kr_summed, 1)
            dve.wait_ge(kr_summed, 1)
            rotate(sqs[:, 0, :], 1, sqs[:, 2, :], sqs[:, 1, :], kr_prod)
            dve.wait_ge(kr_prod, 3)
            dve.tensor_tensor(sqs[0:ROPE, 2, :], sqs[0:ROPE, 2, :], sqs[0:ROPE, 1, :], ALU.add).then_inc(kr_rot, 1)
            dve.wait_ge(kr_hi, 1)
            dve.tensor_tensor(krl[0:ROPE, :], sqs[0:ROPE, 2, :], krh[0:ROPE, :].bitcast(F32),
                              ALU.subtract).then_inc(kr_lo, 1)

            def low_of(dst, full, high, have, n, s):
                dve.wait_ge(have, n)
                dve.tensor_tensor(dst, full, high.bitcast(F32), ALU.subtract).then_inc(s, 1)

            def take_statistics(t, n, added):
                dve.wait_ge(out_added, added)
                dve.bn_stats(stat[:, t, n, :], res[:, t, n * 512:(n + 1) * 512]).then_inc(stats_taken, 1)

            def add_tile(t, n, m, stage):
                if t < TT - 1:
                    dve.wait_ge(out_done, 12 * m + 3 * n + t + 1)
                else:
                    wait_stage(dve, stage_used, stage)
                block_ = res[:, t, n * 512:(n + 1) * 512]
                dve.tensor_tensor(block_, block_, ps[t][:], ALU.add).then_inc(out_added, 1)

            def add_out(stage, m, then=None, blocks=NB, stats=False):
                then = then or (lambda n: after(ahead(stage, n)))
                for n in range(blocks):
                    then(2 * n)
                    for t in range(TT):
                        add_tile(t, n, m, ahead(stage, 2 * n + 1))
                        if stats:
                            take_statistics(t, n, 16 * m + 4 * n + t + 1)
                    then(2 * n + 1)

            def variance(t, taken):
                dve.wait_ge(stats_taken, taken)
                dve.bn_aggr(mv[:, t, :], stat[:, t, :, :].rearrange("p n s -> p (n s)")).then_inc(var_ready, 1)

            def scaling(norm, t):
                dve.wait_ge(std_ready, TT * norm + t + 1)
                dve.reciprocal(rstd[:, t:t + 1], std[:, t:t + 1]).then_inc(rstd_ready, 1)
                dve.wait_ge(rstd_ready, TT * norm + t + 1)
                dve.scalar_tensor_tensor(shift[:, t:t + 1], mv[:, t, 0:1], -1.0, rstd[:, t:t + 1],
                                         ALU.mult, ALU.mult).then_inc(shift_ready, 1)

            def heads(base, i, table, first):
                dve.tensor_copy(cw[:], vec[:, CW:CW + K * 8].rearrange("p (k h) -> p k h", k=K)[
                    :, :, bass.ds(2 * i, 2)]).then_inc(cw_ready, 1)
                for hh, at in enumerate(table):
                    head = 2 * i + hh

                    def st(name, n=0):
                        return ahead(base, at[name] + n)
                    after(st("c"))
                    after(st("c", 1))
                    if not (first and hh == 0):
                        low_of(ml[:, 2 * (1 - hh), :], ps[B_PV][:], mh[:, 2 * (1 - hh), :], pv_hi, head, pv_lo)
                    low_of(knl, ps[B_KN][:], knh, kn_hi, head + 1, kn_lo)
                    if hh == 0:
                        for n in range(2):
                            low_of(vals[:, 2 + n, :], ps[B_V[n]][:], vals[:, n, :], v_hi, head + n + 1, v_lo)
                    after(st("ukv"))
                    wait_stage(dve, stage_used, st("uq"))
                    if hh == 0:
                        rotate(ps[B_QR], 2, tmp_a, tmp_b, qr_prod)
                        dve.wait_ge(qr_prod, 5 * i + 5)
                        for n, (first_row, dst) in enumerate(((0, tmp_a), (ROPE, tmp_b))):
                            if n == 1:
                                dve.wait_ge(qr_rot, head + 1)
                            rows_ = slice(first_row, first_row + ROPE)
                            dve.tensor_tensor(dst[0:ROPE, :], tmp_a[rows_, :], tmp_b[rows_, :],
                                              ALU.add).then_inc(qr_rot, 1)
                    low_of(qnl, ps[B_QN][:], qnh, qn_hi, head + 1, qn_lo)
                    if hh == 0:
                        for n in range(2):
                            low_of(qp[n][ROPE:P, :], (tmp_a, tmp_b)[n][0:ROPE, :], qp[n][0:ROPE, :],
                                   qr_hi, head + n + 1, qr_lo)
                    after(st("uq"))
                    if "out" in at:
                        dve.wait_ge(x_scaled, TT)
                        add_out(st("out"), i - 1)
                    after(st("x"))
                    wait_stage(dve, stage_used, st("x", 1))
                    dve.wait_ge(c_copied, head + 1)
                    dve.wait_ge(qr_lo, 2 * i + 2)
                    dve.tensor_tensor(tmp_a, ps[B_X][:], c_sb, ALU.mult).then_inc(x_used, 1)
                    dve.wait_ge(x_used, head + 1)
                    dve.wait_ge(cw_ready, i + 1)
                    dve.tensor_scalar(tmp_b, tmp_a, cw[:, 2, hh:hh + 1], None, ALU.mult).then_inc(conv_tap, 1)
                    for n, back in ((0, 2), (1, 1)):
                        dve.wait_ge(conv_tap, 3 * head + n + 1)
                        dve.scalar_tensor_tensor(tmp_b[:, back:], tmp_a[:, :SEQ - back], cw[:, n, hh:hh + 1],
                                                 tmp_b[:, back:], ALU.mult, ALU.add).then_inc(conv_tap, 1)
                    after(st("x", 1))
                    for j in range(TT):
                        dve.wait_ge(score_done, 4 * head + j + 1)
                        diagonal = ps[j][:, j * P:(j + 1) * P]
                        dve.tensor_tensor(diagonal, diagonal, mask, ALU.add).then_inc(masked, 1)
                    for j in range(TT):
                        dve.wait_ge(masked, 4 * head + j + 1)
                        dve.reduce_max(mx[:, j:j + 1], ps[j][:, 0:(j + 1) * P], AX_X).then_inc(max_taken, 1)
                    dve.wait_ge(max_taken, 4 * head + 4)
                    dve.tensor_scalar(nmx[:], mx[:], -SCALE, None, ALU.mult).then_inc(max_ready, 1)
                    dve.wait_ge(exp_done, 4 * head + 4)
                    dve.reciprocal(rsum[:], psum_p[:]).then_inc(sum_inv, 1)
                    dve.wait_ge(sum_inv, head + 1)
                    for j in range(TT):
                        p_j = prob[:, P_OFF[j]:P_OFF[j + 1]]
                        dve.tensor_scalar(p_j, p_j, rsum[:, j:j + 1], None, ALU.mult).then_inc(p_ready, 1)
                    after(st("b"))
                    wait_stage(dve, stage_used, st("b", 1))
                    dve.wait_ge(conv_tap, 3 * head + 3)
                    dve.tensor_tensor(tmp_a, ps[B_B][:], tmp_b, ALU.mult).then_inc(b_used, 1)
                    after(st("b", 1))
                    low_of(ml[:, 2 * hh + 1, :], tmp_a, mh[:, 2 * hh + 1, :], conv_hi, head + 1, conv_lo)
                    for n in range(3):
                        a, b = PT_OFF[n], PT_OFF[n + 1 if n < 2 else 4]
                        low_of(ptl[:, a:b], ps[B_PT[n]][:, 0:b - a], pth[:, a:b], pt_hi, 3 * head + n + 1, pt_lo)

            heads((S_ITER0, 0), 0, IT0, True)
            with dve.Fori(1, HEADS // 2) as i:
                heads((S_HEADS, i), i, ITN, False)

            def last_out(n):
                if n == 0:
                    low_of(ml[:, 2, :], ps[B_LAST_PV][:], mh[:, 2, :], pv_hi, HEADS, pv_lo)
                if n < 5:
                    after((S_OUT_LAST + n, 0))

            add_out((S_OUT_LAST, 0), HEADS // 2 - 1, last_out, NB - 1, True)

            def last_sum(t):
                m, n = HEADS // 2 - 1, NB - 1
                add_tile(t, n, m, (S_CHUNK0 - 1, 0))
                take_statistics(t, n, 16 * m + 4 * n + t + 1)
                variance(t, 4 * n + t + 1)

            def first_block(t):
                scaling(0, t)
                dve.wait_ge(shift_ready, t + 1)
                block_ = res[:, t, 0:512]
                dve.tensor_scalar(block_, block_, rstd[:, t:t + 1], shift[:, t:t + 1],
                                  ALU.mult, ALU.add).then_inc(normed_dve, 1)

            def norm_full(step):
                k = step % KT
                dve.wait_ge(n_turned, step + 1)
                if step >= 8:
                    dve.wait_ge(*low_made(step - 8))
                dve.tensor_scalar(full[step % 8], turned[step % 4], vec[:, G1 + k:G1 + k + 1],
                                  vec[:, B1 + k:B1 + k + 1], ALU.mult, ALU.add).then_inc(n_full, 1)

            def norm_steps(first, end):
                for step in range(first, end):
                    norm_full(step)
                    if step - 1 in LOW_ON_DVE:
                        low_of(part_of(xl, step - 1), full[(step - 1) % 8], part_of(xh, step - 1), n_hi, step, n_lo)

            last_sum(0)
            split_low((S_CHUNK0, 0))
            first_block(0)
            last_sum(1)
            split_low((S_CHUNK0 + 1, 0))
            first_block(1)
            norm_steps(0, 6)
            split_low((S_CHUNK0 + 2, 0))
            norm_steps(6, 8)
            split_low((S_CHUNK0 + 3, 0))
            norm_steps(8, 10)
            last_sum(2)
            norm_steps(10, 12)
            first_block(2)
            last_sum(3)
            norm_steps(12, 14)
            first_block(3)
            norm_steps(14, STEPS)

            def taps(y, bank, side, q, scaled, tap, conv, n):
                dve.wait_ge(scaled, n + 1)
                for k, back, s in ((0, 2, tap), (1, 1, conv)):
                    if k == 1:
                        dve.wait_ge(tap, n + 1)
                    dve.scalar_tensor_tensor(y[:, back:], ps[bank][:, :SEQ - back], fw[:, k, side, q:q + 1],
                                             y[:, back:], ALU.mult, ALU.add).then_inc(s, 1)

            def gates(stage, q, c, banks, crossed=False):
                g_end = 2 if crossed else 1
                for n in range(1 if crossed else 0, g_end):
                    after(ahead(stage, n))
                taps(yg, banks[0], 0, q, g_scaled, g_tap, g_conv, 4 * c + q)
                for n in range(g_end, 3):
                    after(ahead(stage, n))
                taps(yu, banks[1], 1, q, u_scaled, u_tap, u_conv, 4 * c + q)
                dve.wait_ge(u_conv, 4 * c + q + 1)
                dve.wait_ge(silu_done, 4 * c + q + 1)
                dve.tensor_tensor(a_f, sg, yu, ALU.mult).then_inc(act_full, 1)
                after(ahead(stage, 3))

            def act_low(q, c, high=mh, low=ml):
                low_of(low[:, q, :], a_f, high[:, q, :], act_hi, 4 * c + q + 1, act_lo)

            def chunk_taps(c):
                dve.tensor_copy(fw[:], fcw[:].rearrange("p k (g f) -> p k g f", g=2)[
                    :, :, :, bass.ds(4 * c, 4)]).then_inc(fw_ready, 1)
                dve.wait_ge(fw_ready, c + 1)

            chunk_taps(0)
            for q in range(4):
                gates((S_CHUNK0 + 4 * q, 0), q, 0, pair_banks(q, q == 0), q == 0)
                act_low(q, 0)
            with dve.Fori(1, CHUNKS - 1) as c:
                chunk_taps(c)
                gates((S_CHUNKS, c), 0, c, pair_banks(0))
                dve.wait_ge(res_ready, TT)
                add_out((S_CHUNKS + 4, c), c - 1 + HEADS // 2)
                act_low(0, c)
                for q in range(1, 4):
                    gates((S_CHUNKS + 8 + 4 * q, c), q, c, pair_banks(q))
                    act_low(q, c)
            chunk_taps(CHUNKS - 1)
            for q in range(4):
                gates((S_LAST_CHUNK + 4 * q, 0), q, CHUNKS - 1, pair_banks(q))
                act_low(q, CHUNKS - 1, mh2, ml2)

            def beside(n):
                for stage in beside_last(n):
                    split_low(stage)
            add_out((S_LAST_CHUNK + 16, 0), CHUNKS - 2 + HEADS // 2, beside)

            dve.wait_ge(gb_landed, 64)

            def gain(t, n):
                block_ = res[:, t, n * 512:(n + 1) * 512]
                dve.wait_ge(out_normed, 4 * t + n + 1)
                dve.tensor_tensor(block_, block_, gb[:, 2, n * 512:(n + 1) * 512], ALU.mult).then_inc(out_gained, 1)

            for t in range(TT):
                for n in range(NB):
                    block_ = res[:, t, n * 512:(n + 1) * 512]
                    dve.wait_ge(last_done, 4 * t + n + 1)
                    dve.tensor_tensor(block_, block_, ps[4 * ((t + 1) % 2) + n][:], ALU.add).then_inc(out_added, 1)
                    take_statistics(t, n, 16 * (CHUNKS - 1 + HEADS // 2) + 4 * t + n + 1)
                    if t > 0 and n < NB - 1:
                        gain(t - 1, n)
                        if n == 2:
                            gain(t - 1, 3)
                variance(t, 16 + 4 * t + 4)
                if t < TT - 1:
                    scaling(1, t)
            t = TT - 1
            dve.wait_ge(var_ready, 2 * TT)
            for n in range(1, NB):
                cols = slice(n * 512, (n + 1) * 512)
                dve.scalar_tensor_tensor(res[:, t, cols], res[:, t, cols], mv[:, t, 0:1], gb[:, 2, cols],
                                         ALU.subtract, ALU.mult).then_inc(out_gained, 1)
                if n == 1:
                    scaling(1, t)
            for n in range(1, NB):
                cols = slice(n * 512, (n + 1) * 512)
                dve.wait_ge(out_gained, 4 * t + n)
                dve.scalar_tensor_tensor(res[:, t, cols], res[:, t, cols], rstd[:, t:t + 1], gb[:, 3, cols],
                                         ALU.mult, ALU.add).then_inc(out_ready_dve, 1)

        @block.gpsimd
        def _(pool):
            pool.wait_ge(xl_ready, 4 * TT)
            for t in range(TT):
                pool.tensor_scalar(res[:, t, :], res[:, t, :], ALPHA, None, ALU.mult).then_inc(x_scaled, 1)
            for step in range(STEPS):
                if step not in LOW_ON_DVE:
                    pool.wait_ge(n_hi, step + 1)
                    pool.tensor_tensor(part_of(xl, step), full[step % 8], part_of(xh, step).bitcast(F32),
                                       ALU.subtract).then_inc(n_lo_pool, 1)
            pool.wait_ge(gb_landed, 64)
            pool.wait_ge(n_turned, STEPS)
            for t in range(TT):
                pool.tensor_tensor(res[:, t, :], res[:, t, :], gb[:, 0, :], ALU.mult).then_inc(res_step, 1)
                pool.wait_ge(res_step, 2 * t + 1)
                pool.tensor_tensor(res[:, t, :], res[:, t, :], gb[:, 1, :], ALU.add).then_inc(res_step, 1)
                pool.wait_ge(res_step, 2 * t + 2)
                pool.tensor_scalar(res[:, t, :], res[:, t, :], ALPHA, None, ALU.mult).then_inc(res_ready, 1)
            for t in range(TT):
                for n in range(NB):
                    if not on_dve(t, n):
                        block_ = res[:, t, n * 512:(n + 1) * 512]
                        if t < TT - 1:
                            pool.wait_ge(out_gained, 4 * t + n + 1)
                        else:
                            pool.wait_ge(out_normed, 4 * t + n + 1)
                            pool.tensor_tensor(block_, block_, gb[:, 2, n * 512:(n + 1) * 512],
                                               ALU.mult).then_inc(res_step, 1)
                            pool.wait_ge(res_step, 2 * TT + 1)
                        pool.tensor_tensor(block_, block_, gb[:, 3, n * 512:(n + 1) * 512],
                                           ALU.add).then_inc(out_ready, 1)


INPUTS = ["x", "positions", "w_in", "q_norm_g", "w_uq", "kv_norm_g", "w_ukv", "conv_w", "w_out", "ln1_g",
          "ln1_b", "w_gate_up", "ffn_conv_w", "w_down", "ln2_g", "ln2_b"]


def kernel(**inputs):
    import concourse.bacc as bacc
    from concourse.bass_utils import run_bass_kernel_spmd

    nc = bacc.Bacc("TRN2", target_bir_lowering=False, num_devices=1, dynamic_dma_scratch_size=1024)
    arrays = {"in_consts": shape_constants()}
    for name in INPUTS:
        arrays[f"in_{name}"] = np.ascontiguousarray(inputs[name])
    args = [nc.dram_tensor(name, a.shape, mybir.dt.from_np(a.dtype), kind="ExternalInput").ap()
            for name, a in arrays.items()]
    out = nc.dram_tensor("out", (1, SEQ, D_MODEL), F32, kind="ExternalOutput").ap()
    hybrid_layer(nc, *args, out)
    r = run_bass_kernel_spmd(nc, [arrays], core_ids=[0])
    return r.results[0]["out"]
```
